# Optimizing a Trainium2 kernel written in Bass

```python
import math
import jax, jax.numpy as jnp
from jax import lax
import numpy as np

D_MODEL = 1024
BATCH = 1
SEQ = 1024
DEPTH = 1

CHUNK = 64
CONV_CH = D_MODEL // 2
CONV_WIDTH = 31
RET_HEADS = 8
RET_DV = (D_MODEL // 2) // RET_HEADS
RET_DK = RET_DV // 2
D_MIX = CONV_CH + RET_HEADS * RET_DV
N_MEM = 256
XATTN_HEADS = 4
XATTN_HEAD_DIM = D_MODEL // XATTN_HEADS
D_FF = 4 * D_MODEL
ROPE_BASE = 10000.0
EPS = 1e-6

IN_SPLITS = (CONV_CH, CONV_CH, RET_HEADS * RET_DK, RET_HEADS * RET_DK, RET_HEADS * RET_DV, RET_HEADS * RET_DV)
D_IN = sum(IN_SPLITS)


def rmsnorm(x, w):
    xf = x.astype(jnp.float32)
    y = xf * lax.rsqrt(jnp.mean(xf * xf, axis=-1, keepdims=True) + EPS)
    return (y * w.astype(jnp.float32)).astype(x.dtype)

def apply_rotary(t, positions):
    half = t.shape[-1] // 2
    inv_freq = ROPE_BASE ** (-jnp.arange(half, dtype=jnp.float32) / half)
    ang = positions.astype(jnp.float32)[..., None] * inv_freq
    cos = jnp.cos(ang)[:, :, None, :]
    sin = jnp.sin(ang)[:, :, None, :]
    t1, t2 = t[..., :half].astype(jnp.float32), t[..., half:].astype(jnp.float32)
    return jnp.concatenate([t1 * cos - t2 * sin, t1 * sin + t2 * cos], axis=-1)

def conv_module(a, b, conv_w, conv_b, ln_w, ln_b):
    u = a * jax.nn.sigmoid(b)
    y = lax.conv_general_dilated(
        u, conv_w[:, None, :], window_strides=(1,), padding=[(CONV_WIDTH - 1, 0)],
        dimension_numbers=("NWC", "WIO", "NWC"), feature_group_count=CONV_CH) + conv_b
    yf = y.astype(jnp.float32)
    mu = jnp.mean(yf, axis=-1, keepdims=True)
    var = jnp.mean(jnp.square(yf - mu), axis=-1, keepdims=True)
    yn = (yf - mu) * lax.rsqrt(var + EPS) * ln_w + ln_b
    return jax.nn.silu(yn)

def retention(q, k, v, positions):
    B, S = q.shape[:2]
    N = S // CHUNK
    q = apply_rotary(q.reshape(B, S, RET_HEADS, RET_DK), positions) * (RET_DK ** -0.5)
    k = apply_rotary(k.reshape(B, S, RET_HEADS, RET_DK), positions)
    v = v.reshape(B, S, RET_HEADS, RET_DV).astype(jnp.float32)
    qc = q.reshape(B, N, CHUNK, RET_HEADS, RET_DK)
    kc = k.reshape(B, N, CHUNK, RET_HEADS, RET_DK)
    vc = v.reshape(B, N, CHUNK, RET_HEADS, RET_DV)

    log_g = jnp.log1p(-jnp.exp2(-5.0 - jnp.arange(RET_HEADS, dtype=jnp.float32)))
    idx = jnp.arange(CHUNK, dtype=jnp.float32)
    dist = jnp.abs(idx[:, None] - idx[None, :])
    decay_in = jnp.exp(log_g[:, None, None] * dist)
    zeta = jnp.exp(log_g[:, None] * (CHUNK - 1 - idx)[None, :])
    xi = jnp.exp(log_g[:, None] * (idx + 1.0)[None, :])
    g_chunk = jnp.exp(log_g * CHUNK)

    scores = jnp.einsum('bnihd,bnjhd->bnhij', qc, kc) * decay_in
    y_in = jnp.einsum('bnhij,bnjhe->bnihe', scores, vc)

    kv = jnp.einsum('bnjhd,bnjhe,hj->nbhde', kc, vc, zeta)

    def step(state, kv_n):
        return g_chunk[None, :, None, None] * state + kv_n, state

    init = jnp.zeros((B, RET_HEADS, RET_DK, RET_DV), jnp.float32)
    _, state_prev = lax.scan(step, init, kv)
    y_x = jnp.einsum('bnihd,nbhde,hi->bnihe', qc, state_prev, xi)
    return (y_in + y_x).reshape(B, S, RET_HEADS, RET_DV)

def head_group_mixer(h, positions, w_in, conv_w, conv_b, conv_ln_w, conv_ln_b, ret_gn_w, w_out):
    B, S, _ = h.shape
    proj = h @ w_in
    cuts = list(np.cumsum(IN_SPLITS)[:-1])
    ca, cb, rq, rk, rv, rg = jnp.split(proj, cuts, axis=-1)
    y_conv = conv_module(ca, cb, conv_w, conv_b, conv_ln_w, conv_ln_b)
    y = retention(rq, rk, rv, positions)
    mu = jnp.mean(y, axis=-1, keepdims=True)
    var = jnp.mean(jnp.square(y - mu), axis=-1, keepdims=True)
    y = (y - mu) * lax.rsqrt(var + EPS) * ret_gn_w.reshape(RET_HEADS, RET_DV)
    y_ret = jax.nn.silu(rg.astype(jnp.float32)) * y.reshape(B, S, RET_HEADS * RET_DV)
    merged = jnp.concatenate([y_conv, y_ret], axis=-1).astype(h.dtype)
    return merged @ w_out

def memory_cross_attention(h, mem_n, xq_w, xkv_w, xo_w):
    B, S, _ = h.shape
    q = (h @ xq_w).reshape(B, S, XATTN_HEADS, XATTN_HEAD_DIM)
    kv = (mem_n @ xkv_w).reshape(B, N_MEM, 2, XATTN_HEADS, XATTN_HEAD_DIM)
    k, v = kv[:, :, 0], kv[:, :, 1]
    s = jnp.einsum('bshd,bmhd->bhsm', q.astype(jnp.float32), k.astype(jnp.float32)) * (XATTN_HEAD_DIM ** -0.5)
    p = jax.nn.softmax(s, axis=-1)
    o = jnp.einsum('bhsm,bmhd->bshd', p, v.astype(jnp.float32)).reshape(B, S, D_MODEL)
    return o.astype(h.dtype) @ xo_w

def sq_relu_mlp(h, up_w, down_w):
    return jnp.square(jax.nn.relu(h @ up_w)) @ down_w

def first_inputs(seed: int = 0) -> dict:
    key = jax.random.key(seed)
    ks = jax.random.split(key, 24)
    f32 = jnp.float32

    def w(k, shape, fan_in):
        return jax.random.normal(k, shape, f32) * (fan_in ** -0.5)

    def gain(k, n):
        return 1.0 + 0.02 * jax.random.normal(k, (n,), f32)

    x = jax.random.normal(ks[0], (BATCH, SEQ, D_MODEL), f32)
    mem = jax.random.normal(ks[1], (BATCH, N_MEM, D_MODEL), f32)
    start = jax.random.randint(ks[2], (BATCH, 1), 0, 1000, dtype=jnp.int32) * CHUNK
    positions = (start + jnp.arange(SEQ, dtype=jnp.int32)[None, :]).astype(jnp.int32)
    return {
        "x": x,
        "mem": mem,
        "positions": positions,
        "norm_mix_w": gain(ks[3], D_MODEL),
        "w_in": w(ks[4], (D_MODEL, D_IN), D_MODEL),
        "conv_w": w(ks[5], (CONV_WIDTH, CONV_CH), CONV_WIDTH),
        "conv_b": 0.02 * jax.random.normal(ks[6], (CONV_CH,), f32),
        "conv_ln_w": gain(ks[7], CONV_CH),
        "conv_ln_b": 0.02 * jax.random.normal(ks[8], (CONV_CH,), f32),
        "ret_gn_w": gain(ks[9], RET_HEADS * RET_DV),
        "w_out": w(ks[10], (D_MIX, D_MODEL), D_MIX),
        "norm_xattn_w": gain(ks[11], D_MODEL),
        "norm_mem_w": gain(ks[12], D_MODEL),
        "xq_w": w(ks[13], (D_MODEL, D_MODEL), D_MODEL),
        "xkv_w": w(ks[14], (D_MODEL, 2 * D_MODEL), D_MODEL),
        "xo_w": w(ks[15], (D_MODEL, D_MODEL), D_MODEL),
        "norm_mlp_w": gain(ks[16], D_MODEL),
        "mlp_up_w": w(ks[17], (D_MODEL, D_FF), D_MODEL),
        "mlp_down_w": w(ks[18], (D_FF, D_MODEL), D_FF),
        "norm_f_w": gain(ks[19], D_MODEL),
    }

def first_block(x, mem, positions, norm_mix_w, w_in, conv_w, conv_b, conv_ln_w, conv_ln_b, ret_gn_w, w_out,
              norm_xattn_w, norm_mem_w, xq_w, xkv_w, xo_w, norm_mlp_w, mlp_up_w, mlp_down_w, norm_f_w):
    h = x
    mem_n = rmsnorm(mem, norm_mem_w)
    for _ in range(DEPTH):
        h = h + head_group_mixer(rmsnorm(h, norm_mix_w), positions, w_in, conv_w, conv_b,
                                 conv_ln_w, conv_ln_b, ret_gn_w, w_out)
        h = h + memory_cross_attention(rmsnorm(h, norm_xattn_w), mem_n, xq_w, xkv_w, xo_w)
        h = h + sq_relu_mlp(rmsnorm(h, norm_mlp_w), mlp_up_w, mlp_down_w)
    return rmsnorm(h, norm_f_w).astype(x.dtype)


GRID_W = 64
CTX_LEN = 256
N_HEADS = 8
N_KV_HEADS = 2
HEAD_DIM = 64
GQA_GROUP = N_HEADS // N_KV_HEADS
ATT_WIDTH = N_HEADS * HEAD_DIM
KV_WIDTH = N_KV_HEADS * HEAD_DIM
CONV_WIDTH_2 = D_MODEL - ATT_WIDTH
CONV_GROUPS = 8
CONV_K = 3
WINDOW = 128
BLOCK = 128
ROPE_THETA = 10000.0
N_EXPERTS = 16
EC_CAPACITY_FACTOR = 2
D_EXPERT = 1024
IN_WIDTH = ATT_WIDTH + 2 * KV_WIDTH + 3 * CONV_WIDTH_2
SPLIT_POINTS = [ATT_WIDTH, ATT_WIDTH + KV_WIDTH, ATT_WIDTH + 2 * KV_WIDTH,
                ATT_WIDTH + 2 * KV_WIDTH + CONV_WIDTH_2, ATT_WIDTH + 2 * KV_WIDTH + 2 * CONV_WIDTH_2]


def rmsnorm_2(x, g):
    xf = x.astype(jnp.float32)
    r = xf * lax.rsqrt(jnp.mean(xf * xf, axis=-1, keepdims=True) + EPS)
    return (r * g.astype(jnp.float32)).astype(x.dtype)

def modulate(h, shift, scale):
    return h * (1 + scale) + shift

def axial_rope_tables(seq_len):
    rows = seq_len // GRID_W
    row = jnp.repeat(jnp.arange(rows), GRID_W, total_repeat_length=rows * GRID_W)
    col = jnp.tile(jnp.arange(GRID_W), rows)
    n_freq = HEAD_DIM // 4
    inv = ROPE_THETA ** (-jnp.arange(n_freq, dtype=jnp.float32) / n_freq)
    ang = jnp.concatenate([row.astype(jnp.float32)[:, None] * inv,
                           col.astype(jnp.float32)[:, None] * inv], axis=-1)
    return jnp.cos(ang), jnp.sin(ang)

def apply_rope(x, cos, sin):
    xf = x.astype(jnp.float32)
    half = HEAD_DIM // 2
    x1, x2 = xf[..., :half], xf[..., half:]
    cs, sn = cos[None, :, None, :], sin[None, :, None, :]
    return jnp.concatenate([x1 * cs - x2 * sn, x1 * sn + x2 * cs], axis=-1).astype(x.dtype)

def windowed_attention(q, k, v, k_ctx, v_ctx, sink):
    bsz, seq, _, hd = q.shape
    nb = seq // BLOCK
    scale = hd ** -0.5
    qb = q.reshape(bsz, nb, BLOCK, N_KV_HEADS, GQA_GROUP, hd)
    pad = ((0, 0), (BLOCK, BLOCK), (0, 0), (0, 0))
    kp = jnp.pad(k, pad).reshape(bsz, nb + 2, BLOCK, N_KV_HEADS, hd)
    vp = jnp.pad(v, pad).reshape(bsz, nb + 2, BLOCK, N_KV_HEADS, hd)
    kb = jnp.concatenate([kp[:, :-2], kp[:, 1:-1], kp[:, 2:]], axis=2)
    vb = jnp.concatenate([vp[:, :-2], vp[:, 1:-1], vp[:, 2:]], axis=2)
    s_loc = jnp.einsum('bnqkgd,bnjkd->bnkgqj', qb, kb).astype(jnp.float32) * scale
    s_ctx = jnp.einsum('bnqkgd,bjkd->bnkgqj', qb, k_ctx).astype(jnp.float32) * scale
    i = jnp.arange(BLOCK)[None, :, None]
    j = jnp.arange(3 * BLOCK)[None, None, :]
    kpos = jnp.arange(nb)[:, None, None] * BLOCK + j - BLOCK
    valid = (jnp.abs(j - BLOCK - i) <= WINDOW) & (kpos >= 0) & (kpos < seq)
    s_loc = jnp.where(valid[None, :, None, None], s_loc, -jnp.inf)
    sk = jnp.broadcast_to(sink.astype(jnp.float32).reshape(N_KV_HEADS, GQA_GROUP)[None, None, :, :, None, None],
                          s_loc.shape[:-1] + (1,))
    p = jax.nn.softmax(jnp.concatenate([sk, s_ctx, s_loc], axis=-1), axis=-1)
    n_ctx = k_ctx.shape[1]
    p_ctx = p[..., 1:1 + n_ctx].astype(v.dtype)
    p_loc = p[..., 1 + n_ctx:].astype(v.dtype)
    out = (jnp.einsum('bnkgqj,bjkd->bnqkgd', p_ctx, v_ctx)
           + jnp.einsum('bnkgqj,bnjkd->bnqkgd', p_loc, vb))
    return out.reshape(bsz, seq, N_HEADS * hd)

def context_attention(q, k, v, sink):
    bsz, n, _, hd = q.shape
    qg = q.reshape(bsz, n, N_KV_HEADS, GQA_GROUP, hd)
    s = jnp.einsum('bqkgd,bjkd->bkgqj', qg, k).astype(jnp.float32) * hd ** -0.5
    sk = jnp.broadcast_to(sink.astype(jnp.float32).reshape(N_KV_HEADS, GQA_GROUP)[None, :, :, None, None],
                          s.shape[:-1] + (1,))
    p = jax.nn.softmax(jnp.concatenate([sk, s], axis=-1), axis=-1)[..., 1:].astype(v.dtype)
    return jnp.einsum('bkgqj,bjkd->bqkgd', p, v).reshape(bsz, n, N_HEADS * hd)

def short_conv_mixer(bg, cg, hv, conv_w):
    u = cg * hv
    up = jnp.pad(u, ((0, 0), (1, 1), (0, 0)))
    y = conv_w[0] * up[:, :-2] + conv_w[1] * up[:, 1:-1] + conv_w[2] * up[:, 2:]
    return bg * y

def expert_choice_ffn(h, w_router, w_gate, w_up, w_down):
    bsz, n, d = h.shape
    cap = EC_CAPACITY_FACTOR * n // N_EXPERTS
    aff = jax.nn.softmax((h @ w_router).astype(jnp.float32), axis=-1)
    g, idx = lax.top_k(jnp.swapaxes(aff, 1, 2), cap)
    xs = jax.vmap(lambda hb, ib: hb[ib])(h, idx)
    a = jnp.einsum('becd,edf->becf', xs, w_gate)
    u = jnp.einsum('becd,edf->becf', xs, w_up)
    y = jnp.einsum('becf,efd->becd', jax.nn.silu(a) * u, w_down) * g[..., None].astype(h.dtype)
    flat = (idx + (jnp.arange(bsz) * n)[:, None, None]).reshape(-1)
    out = jax.ops.segment_sum(y.reshape(-1, d), flat, num_segments=bsz * n)
    return out.reshape(bsz, n, d)

def second_inputs(seed: int = 0) -> dict:
    key = jax.random.key(seed)
    ks = jax.random.split(key, 17)
    D = D_MODEL
    nrm = jax.random.normal
    f32 = jnp.float32
    return {
        "x": nrm(ks[0], (BATCH, SEQ, D), f32),
        "c": nrm(ks[1], (BATCH, D), f32),
        "ctx": nrm(ks[2], (BATCH, CTX_LEN, D), f32),
        "c_ctx": nrm(ks[3], (D,), f32),
        "w_ada": nrm(ks[4], (DEPTH, D, 6 * D), f32) * (0.5 * D ** -0.5),
        "b_ada": nrm(ks[5], (DEPTH, 6 * D), f32) * 0.01,
        "g_mix": 1.0 + 0.1 * nrm(ks[6], (DEPTH, D), f32),
        "w_in": nrm(ks[7], (DEPTH, D, IN_WIDTH), f32) * D ** -0.5,
        "conv_w": nrm(ks[8], (DEPTH, CONV_K, CONV_WIDTH_2), f32) * CONV_K ** -0.5,
        "sink": nrm(ks[9], (DEPTH, N_HEADS), f32),
        "w_out": nrm(ks[10], (DEPTH, D, D), f32) * D ** -0.5,
        "g_ffn": 1.0 + 0.1 * nrm(ks[11], (DEPTH, D), f32),
        "w_router": nrm(ks[12], (DEPTH, D, N_EXPERTS), f32) * D ** -0.5,
        "w_gate": nrm(ks[13], (DEPTH, N_EXPERTS, D, D_EXPERT), f32) * D ** -0.5,
        "w_up": nrm(ks[14], (DEPTH, N_EXPERTS, D, D_EXPERT), f32) * D ** -0.5,
        "w_down": nrm(ks[15], (DEPTH, N_EXPERTS, D_EXPERT, D), f32) * D_EXPERT ** -0.5,
        "g_final": 1.0 + 0.1 * nrm(ks[16], (D,), f32),
    }

def second_block(x, c, ctx, c_ctx, w_ada, b_ada, g_mix, w_in, conv_w, sink, w_out, g_ffn,
              w_router, w_gate, w_up, w_down, g_final):
    bsz, seq, _ = x.shape
    cos, sin = axial_rope_tables(seq)
    for l in range(DEPTH):
        last = l == DEPTH - 1
        mod = jax.nn.silu(c) @ w_ada[l] + b_ada[l]
        sh1, sc1, gt1, sh2, sc2, gt2 = [m[:, None, :] for m in jnp.split(mod, 6, axis=-1)]
        mod_c = jax.nn.silu(c_ctx) @ w_ada[l] + b_ada[l]
        csh1, csc1, cgt1, csh2, csc2, cgt2 = jnp.split(mod_c, 6, axis=-1)

        hc = modulate(rmsnorm_2(ctx, g_mix[l]), csh1, csc1)
        n_ctx = ctx.shape[1]
        if last:
            kv_c = hc @ w_in[l][:, ATT_WIDTH:ATT_WIDTH + 2 * KV_WIDTH]
            k_c, v_c = jnp.split(kv_c, 2, axis=-1)
            k_c = k_c.reshape(bsz, n_ctx, N_KV_HEADS, HEAD_DIM)
            v_c = v_c.reshape(bsz, n_ctx, N_KV_HEADS, HEAD_DIM)
        else:
            q_c, k_c, v_c, bg_c, cg_c, hv_c = jnp.split(hc @ w_in[l], SPLIT_POINTS, axis=-1)
            q_c = q_c.reshape(bsz, n_ctx, N_HEADS, HEAD_DIM)
            k_c = k_c.reshape(bsz, n_ctx, N_KV_HEADS, HEAD_DIM)
            v_c = v_c.reshape(bsz, n_ctx, N_KV_HEADS, HEAD_DIM)
            att_c = context_attention(q_c, k_c, v_c, sink[l])
            conv_c = short_conv_mixer(bg_c, cg_c, hv_c, conv_w[l])
            ctx_new = ctx + cgt1 * (jnp.concatenate([att_c, conv_c], axis=-1) @ w_out[l])
            hc2 = modulate(rmsnorm_2(ctx_new, g_ffn[l]), csh2, csc2)
            ctx_new = ctx_new + cgt2 * expert_choice_ffn(hc2, w_router[l], w_gate[l], w_up[l], w_down[l])

        h = modulate(rmsnorm_2(x, g_mix[l]), sh1, sc1)
        q, k, v, bg, cg, hv = jnp.split(h @ w_in[l], SPLIT_POINTS, axis=-1)
        q = apply_rope(q.reshape(bsz, seq, N_HEADS, HEAD_DIM), cos, sin)
        k = apply_rope(k.reshape(bsz, seq, N_KV_HEADS, HEAD_DIM), cos, sin)
        v = v.reshape(bsz, seq, N_KV_HEADS, HEAD_DIM)
        att = windowed_attention(q, k, v, k_c, v_c, sink[l])
        conv = short_conv_mixer(bg, cg, hv, conv_w[l])
        x = x + gt1 * (jnp.concatenate([att, conv], axis=-1) @ w_out[l])

        h2 = modulate(rmsnorm_2(x, g_ffn[l]), sh2, sc2)
        x = x + gt2 * expert_choice_ffn(h2, w_router[l], w_gate[l], w_up[l], w_down[l])

        if not last:
            ctx = ctx_new
    return rmsnorm_2(x, g_final)


def setup_inputs(seed=0):
    out = dict(first_inputs(seed))
    for name, value in second_inputs(seed + 1).items():
        if name != "x":
            out[name + "_2"] = value
    return out


def reference(
    x, mem, positions, norm_mix_w, w_in, conv_w, conv_b, conv_ln_w, conv_ln_b, ret_gn_w, w_out,
    norm_xattn_w, norm_mem_w, xq_w, xkv_w, xo_w, norm_mlp_w, mlp_up_w, mlp_down_w, norm_f_w,
    c_2, ctx_2, c_ctx_2, w_ada_2, b_ada_2, g_mix_2, w_in_2, conv_w_2, sink_2, w_out_2, g_ffn_2,
    w_router_2, w_gate_2, w_up_2, w_down_2, g_final_2,
):
    x = first_block(
        x, mem, positions, norm_mix_w, w_in, conv_w, conv_b, conv_ln_w, conv_ln_b, ret_gn_w,
        w_out, norm_xattn_w, norm_mem_w, xq_w, xkv_w, xo_w, norm_mlp_w, mlp_up_w, mlp_down_w,
        norm_f_w,
    )
    return second_block(
        x, c_2, ctx_2, c_ctx_2, w_ada_2, b_ada_2, g_mix_2, w_in_2, conv_w_2, sink_2, w_out_2,
        g_ffn_2, w_router_2, w_gate_2, w_up_2, w_down_2, g_final_2,
    )


_drawn_inputs = setup_inputs


def setup_inputs(seed=0):
    import zlib

    import numpy as np

    out = dict(_drawn_inputs(seed))
    spreads = {}
    factors = {'norm_mix_w': 2.868,
     'conv_b': 3.204,
     'conv_ln_w': 5.297,
     'conv_ln_b': 6.616,
     'ret_gn_w': 6.232,
     'norm_xattn_w': 8.0,
     'norm_mem_w': 8.0,
     'norm_mlp_w': 3.073,
     'ctx_2': 3.867,
     'b_ada_2': 4.615,
     'sink_2': 8.0,
     'g_ffn_2': 3.066}
    for name, (base, spread) in spreads.items():
        noise = np.random.default_rng([zlib.crc32(name.encode()), seed]).standard_normal(out[name].shape)
        drawn = base * np.exp(spread * noise) if base else spread * noise
        out[name] = __import__('jax').numpy.asarray(drawn.astype(out[name].dtype))
    for name, factor in factors.items():
        out[name] = (out[name] * factor).astype(out[name].dtype)
    return out
```

```python
from contextlib import ExitStack

import numpy as np

import concourse.bass as bass
from concourse import mybir
from concourse.alu_op_type import AluOpType as ALU

ACT = mybir.ActivationFunctionType
F32 = mybir.dt.float32
F32R = mybir.dt.float32r
BF16 = mybir.dt.bfloat16
I32 = mybir.dt.int32
U32 = mybir.dt.uint32
AX = mybir.AxisListType.X

P = 128
S = 1024
D = 1024
NT = S // P
KT = D // P
CC = 512
TAPS = 31
PADT = TAPS - 1
TAPS_QK, TAPS_VG = 3, 21
HR, DK, DV = 8, 32, 64
MEM = 256
XH, XD = 4, 256
FF = 4096
FB = 512
NFB = FF // FB
AH_, AD = 8, 64
CTX = 256
NE, CAP = 16, 128
EPS = 1e-6
BIG = -1e30
MAGIC = 12582912.0

CI = 0
CO = CI + P
CF = CO + P
CM = CF + 16
CC2 = CM + 2 * P
CPERS = CC2 + 2 * NT * 32
RM = 0
RX = RM + HR * P
RB = RX + 2 * P
RQ = RB + 2 * 4 * DV
RZ = RQ + 4
RG = RZ + HR
RPERS = RG + 2


def shape_constants():
    c = np.zeros((P, CPERS), np.float32)
    c[:, CI:CI + P] = np.eye(P)
    c[:, CO:CO + P] = 1.0 / CC
    c[:, CF:CF + 16] = (10000.0 ** (-np.arange(16) / 16.0)).astype(np.float32)
    i = np.arange(P)
    c[:, CM:CM + P] = np.where(i[None, :] >= i[:, None], 0.0, BIG)
    c[:, CM + P:CM + 2 * P] = np.where(i[None, :] <= i[:, None], 0.0, BIG)
    tok = np.arange(S)
    inv = (10000.0 ** (-np.arange(16) / 16.0)).astype(np.float32)
    ang = np.concatenate([(tok // 64).astype(np.float32)[:, None] * inv,
                          (tok % 64).astype(np.float32)[:, None] * inv], 1).astype(np.float64)
    for n, f in enumerate((np.cos, np.sin)):
        t = f(ang).reshape(NT, P, 32).transpose(1, 0, 2).reshape(P, NT * 32)
        c[:, CC2 + n * NT * 32:CC2 + (n + 1) * NT * 32] = t
    r = np.zeros((P, RPERS), np.float64)
    g = 1.0 - 2.0 ** (-5.0 - np.arange(HR))
    scale = DK ** -0.5
    for h in range(HR):
        m = g[h] ** np.abs(i[:, None] - i[None, :]) * ((i[:, None] // 64) <= (i[None, :] // 64))
        r[:, RM + h * P:RM + (h + 1) * P] = m * scale
        rows = slice(32 * (h % 4), 32 * (h % 4) + 32)
        r[rows, RX + (h // 4) * P:RX + (h // 4 + 1) * P] = scale * g[h] ** (i + 1.0)
        r[rows, RB + h * DV:RB + (h + 1) * DV] = 1.0
        r[rows, RQ + h % 4] = 1.0
        r[:, RZ + h] = g[h] ** (P - 1.0 - i)
        r[rows, RG + h // 4] = g[h] ** P
    return c, r.astype(np.float32)


def build(nc, x, mem, positions, norm_mix_w, w_in, conv_w, conv_b, conv_ln_w, conv_ln_b, ret_gn_w, w_out,
          norm_xattn_w, norm_mem_w, xq_w, xkv_w, xo_w, norm_mlp_w, mlp_up_w, mlp_down_w, norm_f_w,
          c_2, ctx_2, c_ctx_2, w_ada_2, b_ada_2, g_mix_2, w_in_2, conv_w_2, sink_2, w_out_2, g_ffn_2,
          w_router_2, w_gate_2, w_up_2, w_down_2, g_final_2, consts, rconsts, out):
    mod_d = nc.dram_tensor("mod_rows", (2, 6 * D), F32, kind="Internal").ap()
    xsave_d = nc.dram_tensor("x_between_blocks", (S, D), F32, kind="Internal").ap()
    h2_d = nc.dram_tensor("expert_tokens", (S, D), F32, kind="Internal").ap()
    acc_d = nc.dram_tensor("expert_sums", (S, D), F32, kind="Internal").ap()

    BASE = 16512
    K = 1024
    O_RAW, O_WH, O_WL = BASE, BASE + 16 * K, BASE + 32 * K
    O_AH, O_AL = BASE + 48 * K, BASE + 80 * K
    O_R = BASE + 112 * K
    O_S = O_R + 80 * K + 512
    O_T = O_S + 7 * K + 256

    def at(name, shape, dt, off):
        return nc.alloc_sbuf_tensor_at(name, shape, dt, offset=off)

    raw = at("w_raw", [P, 2, 4, 512], F32, O_RAW)
    WH = at("w_hi", [P, 8, 512], F32R, O_WH)
    WL = at("w_lo", [P, 8, 512], F32R, O_WL)
    AH = at("act_hi", [P, 8, S], F32R, O_AH)
    AL = at("act_lo", [P, 8, S], F32R, O_AL)
    X = at("x_tokens", [P, NT, D], F32, O_R + 48 * K + 512)
    XN = at("x_normed", [P, 2, D], F32, O_R + 32 * K + 512)
    GAIN = at("gain_row", [P, D], F32, O_R + 40 * K + 512)
    SHIFT = at("shift_row", [P, D], F32, O_R + 44 * K + 512)

    o = O_S
    CST = at("consts_sb", [P, CPERS], F32, o); o += CPERS * 4
    SS = at("sum_squares", [P, 64], F32, o); o += 256
    SD = at("root_mean_square", [P, 64], F32, o); o += 256
    RS = at("rms_scale", [P, 64], F32, o); o += 256
    VT = at("vectors_T", [P, 4, 37], F32, o); o += 608
    CS = at("silu_c", [P, 2, 8], F32, o); o += 64
    IDB = at("identity_bf16", [P, P], BF16, o); o += 256
    MKB = at("masks_bf16", [P, 2, P], BF16, o); o += 512
    SINK = at("sink_row", [P, 8], F32, o); o += 32
    NSINK = at("minus_sink", [P, 8], F32, o); o += 32
    EPSC = at("eps_col", [P, 1], F32, o); o += 32
    assert o <= O_T, (o, O_T)
    IDN = CST[:, CI:CI + P]
    ONESM = CST[:, CO:CO + P]
    COS2 = CST[:, CC2:CC2 + NT * 32].rearrange("p (t f) -> p t f", t=NT)
    SIN2 = CST[:, CC2 + NT * 32:CC2 + 2 * NT * 32].rearrange("p (t f) -> p t f", t=NT)

    U = at("conv_in", [P, 4, S + PADT], F32, O_R)
    YC = at("conv_out", [P, 4, S], F32, O_R + 16 * K + 512)
    QK = at("ret_qk", [P, NT, 512], F32, O_R + 32 * K + 512)
    V = at("ret_v", [P, NT, 512], F32, O_R + 48 * K + 512)
    G = at("ret_gate", [P, NT, 512], F32, O_R + 64 * K + 512)
    SQ = at("conv_squares", [P, 4, S], F32, O_R)
    SDL = at("conv_ln_rstd", [P, S], F32, O_R + 32 * K + 512)
    o = O_T
    POS = at("pos_i", [P, NT], I32, o); o += 32
    POSF = at("pos_f", [P, NT], F32, o); o += 32
    CS1 = at("cos_sin", [P, 2, NT, 16], F32, o); o += 1024
    RT = at("rope_tmp", [P, 4, 256], F32, o); o += 4096
    o_state = o
    ANG = at("angle", [P, NT, 16], F32, o)
    ANK = at("angle_turns", [P, 2, NT, 16], F32, o + 512)
    STATE = at("ret_state", [P, 2, 256], F32, o_state)
    VEC = at("vector_rows", [37, 512], F32, O_T + 1088)
    BIAS = at("mod_bias", [1, 2, 512], F32, O_T + 1088)
    C8 = at("c_rows", [16, P], F32, O_T + 32 * 2 + 512)
    RC = at("ret_consts", [P, RPERS], F32, O_AH)
    o = O_AH + ((RPERS * 4 + 31) // 32) * 32
    GNW = at("ret_gn_row", [P, 512], F32, o); o += 2048
    YSQ = at("ret_squares", [P, 512], F32, o); o += 2048
    YST = at("ret_stats", [P, 4, 8], F32, o); o += 128
    MODB = at("mod_out", [2, 2, 512], F32, o); o += 4096
    assert o <= O_AH + 16 * K
    o = O_AL
    QBD = at("ret_q_heads", [P, 2, 4, P], F32, o); o += 4096
    KTT = at("ret_k_T", [P, 2, P], F32, o); o += 1024
    QX = at("ret_q_decayed", [P, 2, P], F32, o); o += 1024
    KZ = at("ret_k_decayed", [P, 256], F32, o); o += 1024
    ST = at("ret_scores", [P, 8, P], F32, o); o += 4096
    TKV = at("ret_kv", [P, 2, 256], F32, o); o += 2048
    YD = at("ret_y", [P, 512], F32, o); o += 2048
    assert o <= O_AL + 16 * K

    MTH = at("mem_hi", [P, 8, MEM], F32R, O_R)
    MTL = at("mem_lo", [P, 8, MEM], F32R, O_R + 8 * K)
    MX = at("mem_rows", [P, 2, D], F32, O_R + 16 * K + 512)
    QT = at("x_q_T", [P, 8, S], F32, O_R)
    XM = at("x_max", [P, 16, 2], F32, O_R + 32 * K)
    XL = at("x_sum", [P, 16, 2], F32, O_R + 32 * K + 128)
    KX = at("x_k_T", [P, 8, MEM], F32, O_R + 32 * K + 512)
    VX = at("x_v", [P, 2, D], F32, O_R + 40 * K + 512)
    PX = at("x_probs", [P, 2, 512], F32, O_T)
    PT = at("x_probs_T", [P, 2, 4, P], F32, O_T + 4 * K)
    UH = at("hidden_hi", [P, 4, S], F32R, O_R)
    UL = at("hidden_lo", [P, 4, S], F32R, O_R + 16 * K)
    UF = at("hidden_f32", [P, 2, 512], F32, O_T)
    GF = at("gain_row_final", [P, D], F32, O_T + 4 * K)
    JUNK = at("squares_row", [P, D], F32, O_T)
    GC = at("ctx_gain_row", [P, D], F32, O_R + 24 * K + 512)
    SHC = at("ctx_shift_row", [P, D], F32, O_R + 28 * K + 512)
    QR = at("rotated", [P, 2, 512], F32, O_T)
    RT2 = at("rotary_tmp", [P, 4, 256], F32, O_T + 4 * K)
    QT2 = at("w_q_T", [P, 4, S], F32, O_R + 32 * K + 512)
    KZ4 = at("w_k_T", [P, 4, CTX + S], F32, O_R + 48 * K + 512)
    V2 = at("w_v", [P, 10, P], F32, O_R + 68 * K + 512)
    U2 = at("short_conv_in", [P, 4, S + 2], F32, O_R)
    C2 = at("short_conv_out", [P, 4, S], F32, O_R + 16 * K + 512)
    o = O_R + 73 * K + 512
    OT = at("w_out_rows", [P, 512], F32, o); o += 2048
    M2 = at("w_max", [P, 64], F32, o); o += 256
    NM2 = at("w_minus_max", [P, 64], F32, o); o += 256
    L2 = at("w_sum", [P, 64], F32, o); o += 256
    ES2 = at("w_sink_exp", [P, 64], F32, o); o += 256
    PTB = at("w_probs_T", [P, 640], F32, o); o += 2560
    assert o <= O_S
    P2 = at("w_probs", [P, 2, 640], F32, O_T)
    PTA = at("w_probs_T0", [P, 640], F32, O_T + 5 * K)
    PT2 = [PTA, PTB]
    GT1 = at("gate_row1", [P, D], F32, O_R)
    SCT = at("scale_row", [P, D], F32, O_R + 4 * K)
    T1 = at("gated", [P, 2, 512], F32, O_T)
    HTR = at("router_in_T", [P, 2, 8, P], F32, O_R + 8 * K)
    WR = at("router_w", [P, 8, NE], F32, O_R + 16 * K + 512)
    o = O_R + 17 * K
    RST = at("router_stats", [P, 4, 8], F32, o); o += 128
    REX = at("router_exp", [P, 2, NE], F32, o); o += 128
    AFF = at("affinity", [P, 2, NE], F32, o); o += 128
    AFT = at("affinity_T", [NE, S], F32, o); o += 4096
    TV = at("top_values", [NE, CAP], F32, o); o += 512
    TI = at("top_index", [NE, CAP], U32, o); o += 512
    TIF = at("top_index_f32", [NE, CAP], F32, o); o += 512
    assert o <= O_R + 24 * K
    GV = at("gates", [P, NE], F32, O_R + 23 * K + 512)
    GI = at("token_of_slot", [P, NE], U32, O_R + 23 * K + 576)
    GVC = at("gate_now", [P, 1], F32, O_R + 23 * K + 640)
    EW = [at(f"expert_w{i}", [P, 4, D], F32, O_WH + 16 * K * i) for i in range(6)]
    XS = at("expert_rows", [P, D], F32, O_R + 24 * K)
    XTH = at("expert_rows_T_hi", [P, 8, P], F32R, O_R + 28 * K)
    XTL = at("expert_rows_T_lo", [P, 8, P], F32R, O_T)
    EWH = [at(f"expert_w_hi{i}", [P, 4, D], F32R, a) for i, a in enumerate((O_RAW, O_R + 32 * K + 512, O_R + 64 * K + 512, O_R + 4 * K))]
    EWL = [at(f"expert_w_lo{i}", [P, 4, D], F32R, O_WH + 16 * K * i) for i in range(4)]
    SG = at("expert_silu", [P, D], F32, O_R + 48 * K + 512)
    HE = at("expert_hidden", [P, D], F32, O_R + 52 * K + 512)
    HTE = at("expert_hidden_T", [P, 8, P], F32, O_R + 56 * K + 512)
    YE = at("expert_out", [P, D], F32, O_R + 60 * K + 512)
    GT2 = at("gate_row2", [P, D], F32, O_R)

    PAIR = [nc.alloc_psum_tensor(f"banks{2 * i}{2 * i + 1}", [P, 1024], F32) for i in range(4)]
    BK = [PAIR[i // 2][:, 512 * (i % 2):512 * (i % 2 + 1)] for i in range(8)]

    with ExitStack() as stack:
        def sem(name):
            return stack.enter_context(nc.semaphore(name))

        w_raw = [sem("w_raw0"), sem("w_raw1")]
        w_hi, w_ready, w_used = sem("w_hi_made"), sem("w_ready"), sem("w_used")
        acc_ready, acc_act, acc_dve = sem("acc_ready"), sem("acc_free_act"), sem("acc_free_dve")
        nm_sd, nm_xn, nm_tp, nm_hi, nm_lo = (sem(s) for s in ("nm_sd", "nm_xn", "nm_tp", "nm_hi", "nm_lo"))
        nm_sq = sem("nm_sq")
        cst_in, x_in, vec_in, gain_in = sem("cst_in"), [sem(f"x_in{t}") for t in range(NT)], sem("vec_in"), sem("gain_in")
        dve_link, act_link, pool_link = sem("dve_link"), sem("act_link"), sem("pool_link")
        links = {"dve": 0, "act": 0, "pool": 0}

        def dlink(ins):
            links["dve"] += 1
            ins.then_inc(dve_link, 1)
            nc.vector.wait_ge(dve_link, links["dve"])

        def alink(ins):
            links["act"] += 1
            ins.then_inc(act_link, 1)
            nc.scalar.wait_ge(act_link, links["act"])

        owners = []

        def plan(n, who):
            owners.extend([who] * n)
            return len(owners) - n

        T_CB, T_CA, T_QK, T_V, T_G = plan(8, "a"), plan(8, "d"), plan(8, "d"), plan(8, "a"), plan(8, "a")
        T_WO = plan(16, "d")
        T_MK, T_MV, T_XQ, T_XO = plan(8, "a"), plan(4, "a"), plan(16, "a"), plan(16, "d")
        T_ML = len(owners)
        for _ in range(NFB):
            plan(8, "a")
            plan(16, "d")
        T_Q2, T_KV, T_CG, T_HV, T_BG, T_W2 = (plan(8, "d"), plan(10, "d"), plan(8, "a"), plan(8, "d"),
                                              plan(8, "d"), plan(16, "d"))
        B_IN, B_WO, B_KV, B_XQ, B_XO, B_ML = 0, 5, 7, 11, 13, 15
        B_I2 = B_ML + 2 * NFB
        B_W2 = B_I2 + 5
        LAST = {}
        for b_, n_ in ((B_IN, T_CB + 8), (1, T_CA + 8), (2, T_QK + 8), (3, T_V + 8), (4, T_G + 8), (B_WO, T_WO + 8),
                       (B_WO + 1, T_WO + 16), (B_KV, T_MK + 4), (B_KV + 1, T_MK + 8), (B_KV + 2, T_MV + 2),
                       (B_KV + 3, T_MV + 4), (B_XQ, T_XQ + 8), (B_XQ + 1, T_XQ + 16), (B_XO, T_XO + 8),
                       (B_XO + 1, T_XO + 16), (B_ML, T_ML + 8), (B_ML + 1, T_ML + 24), (B_I2 - 1, T_ML + 24 * NFB),
                       (B_I2, T_Q2 + 8), (B_I2 + 1, T_KV + 10), (B_I2 + 2, T_CG + 8), (B_I2 + 3, T_HV + 8),
                       (B_I2 + 4, T_BG + 8), (B_W2, T_W2 + 8), (B_W2 + 1, T_W2 + 16)):
            LAST[b_] = n_ - 1

        def acc(n):
            return BK[n % 4]

        def freed(n):
            return (acc_act if owners[n] == "a" else acc_dve), owners[:n + 1].count(owners[n])

        def wait_acc_free(n, off=0):
            if n >= 4:
                s, v = freed(n - 4)
                nc.tensor.wait_ge(s, off * (4 if s is acc_act else 8) + v)

        def w_source(b, half):
            def cols(w, lo, n=512):
                return w[:, lo:lo + n].rearrange("(k p) n -> p k n", p=P)[:, 4 * half:4 * half + 4, :], n
            if b < B_WO:
                return cols(w_in, [CC, 0, 2 * CC, 3 * CC, 4 * CC][b])
            if b < B_KV:
                return cols(w_out, 512 * (b - B_WO))
            if b < B_XQ:
                return cols(xkv_w, 512 * (b - B_KV))
            if b < B_XO:
                return cols(xq_w, 512 * (b - B_XQ))
            if b < B_ML:
                return cols(xo_w, 512 * (b - B_XO))
            if b < B_W2:
                return cols(w_in_2[0], [0, 512, 1280, 1792, 768][b - B_I2], 256 if b == B_I2 + 1 else 512)
            return cols(w_out_2[0], 512 * (b - B_W2))

        def sp_load(b, half, src, width=512, when=None):
            if b >= 1:
                nc.sync.wait_ge(w_ready, 4 * (b - 1) + 2 * (half + 1) if when is None else when + 2 * (half + 1))
            nc.sync.dma_start(raw[:, half, :, 0:width], src).then_inc(w_raw[half], 16)

        def split_hi(b, off=0, width=512):
            for j in range(4):
                half = j // 2
                if j % 2 == 0:
                    nc.scalar.wait_ge(w_raw[half], off * 16 + 16 * (b + 1))
                if b >= 1 and j < 3:
                    nc.scalar.wait_ge(w_used, off * 3 + 3 * (b - 1) + j + 1)
                elif b >= 1:
                    nc.scalar.wait_ge(acc_ready, off * 12 + LAST[b - 1] + 1)
                nc.scalar.activation(WH[:, 2 * j:2 * j + 2, 0:width], raw[:, half, 2 * (j % 2):2 * (j % 2) + 2, 0:width],
                                     ACT.Copy).then_inc(w_hi, 1)

        def split_lo(b, off=0, width=512):
            for j in range(4):
                nc.vector.wait_ge(w_hi, off * 4 + 4 * b + j + 1)
                nc.vector.tensor_tensor(WL[:, 2 * j:2 * j + 2, 0:width],
                                        raw[:, j // 2, 2 * (j % 2):2 * (j % 2) + 2, 0:width],
                                        WH[:, 2 * j:2 * j + 2, 0:width], ALU.subtract).then_inc(w_ready, 1)

        def mm3(o_, lh, ll, rh, rl, start, stop):
            nc.tensor.matmul(o_, lh, rh, start=start, stop=False)
            nc.tensor.matmul(o_, lh, rl, start=False, stop=False)
            return nc.tensor.matmul(o_, ll, rh, start=False, stop=stop)

        def tok(t):
            return slice(t * P, (t + 1) * P)

        def gemm_tokens(b, n0, lo=0, hi=NT, before=None, after=None, lhs=None, rhs_cols=(0, 512)):
            for t in range(lo, hi):
                n = n0 + t - lo
                if before:
                    before(t)
                wait_acc_free(n)
                Lh, Ll = lhs(t) if lhs else (AH[:, :, tok(t)], AL[:, :, tok(t)])
                w = rhs_cols[1] - rhs_cols[0]
                for k in range(8):
                    if t == lo and k % 2 == 0:
                        nc.tensor.wait_ge(w_ready, 4 * b + k // 2 + 1)
                    m = mm3(acc(n)[:, 0:w], Lh[:, k, :], Ll[:, k, :], WH[:, k, rhs_cols[0]:rhs_cols[1]],
                            WL[:, k, rhs_cols[0]:rhs_cols[1]], k == 0, k == 7)
                    if t == hi - 1 and k in (1, 3, 5):
                        m.then_inc(w_used, 1)
                m.then_inc(acc_ready, 1)
                if after:
                    after(t)

        def gemm_features(b, n0, before=None, after=None, off=0):
            for m_ in range(8):
                h, c = m_ // 4, m_ % 4
                if before:
                    before(m_)
                wait_acc_free(n0 + m_, off)
                for k in range(8):
                    if m_ == 0 and k % 2 == 0:
                        nc.tensor.wait_ge(w_ready, off * 4 + 4 * b + k // 2 + 1)
                    m = mm3(acc(n0 + m_)[:, :], WH[:, k, c * P:(c + 1) * P], WL[:, k, c * P:(c + 1) * P],
                            AH[:, k, h * 512:(h + 1) * 512], AL[:, k, h * 512:(h + 1) * 512], k == 0, k == 7)
                    if m_ == 7 and k in (1, 3, 5):
                        m.then_inc(w_used, 1)
                m.then_inc(acc_ready, 1)
                if after:
                    after(m_)

        def norm_stats(i, src, junk=None):
            if i >= 2:
                nc.scalar.wait_ge(nm_tp, 2 * (i - 1))
            nc.scalar.activation(XN[:, i % 2, :] if junk is None else junk, src, ACT.Square,
                                 accum_out=SS[:, i:i + 1]).then_inc(nm_sq, 1)
            nc.scalar.wait_ge(nm_sq, i + 1)
            nc.scalar.activation(SD[:, i:i + 1], SS[:, i:i + 1], ACT.Sqrt, bias=EPSC[:, 0:1],
                                 scale=1.0 / D).then_inc(nm_sd, 1)

        def norm_rows(i, src, shift=None, gain=GAIN):
            nc.vector.wait_ge(nm_sd, i + 1)
            dlink(nc.vector.reciprocal(RS[:, i:i + 1], SD[:, i:i + 1]))
            r = nc.vector.scalar_tensor_tensor(out=XN[:, i % 2, :], in0=src, scalar=RS[:, i:i + 1], in1=gain[:, :],
                                               op0=ALU.mult, op1=ALU.mult)
            if shift is not None:
                dlink(r)
                r = nc.vector.tensor_tensor(XN[:, i % 2, :], XN[:, i % 2, :], shift[:, :], ALU.add)
            r.then_inc(nm_xn, 1)

        def norm_transpose(i, banks=4, free=None):
            nc.tensor.wait_ge(nm_xn, i + 1)
            for hb in range(2):
                q = 2 * i + hb
                if q >= 4:
                    nc.tensor.wait_ge(nm_lo if free is None else free, q + 1 - banks)
                for c in range(4):
                    k = 4 * hb + c
                    m = nc.tensor.transpose(BK[4 + q % banks][:, c * P:(c + 1) * P], XN[:, i % 2, k * P:(k + 1) * P], IDN)
                m.then_inc(nm_tp, 1)

        def norm_hi(i, dst):
            for hb in range(2):
                q = 2 * i + hb
                nc.scalar.wait_ge(nm_tp, q + 1)
                nc.scalar.activation(dst[:, 4 * hb:4 * hb + 4, :], BK[4 + q % 4][:, :].rearrange("p (c n) -> p c n", c=4),
                                     ACT.Copy).then_inc(nm_hi, 1)

        def norm_lo(i, hi, dst):
            for hb in range(2):
                q = 2 * i + hb
                nc.vector.wait_ge(nm_hi, q + 1)
                nc.vector.tensor_tensor(dst[:, 4 * hb:4 * hb + 4, :],
                                        BK[4 + q % 4][:, :].rearrange("p (c n) -> p c n", c=4),
                                        hi[:, 4 * hb:4 * hb + 4, :], ALU.subtract).then_inc(nm_lo, 1)

        def a_hi(t):
            return AH[:, :, tok(t)]

        def a_lo(t):
            return AL[:, :, tok(t)]

        def plain_stats(j, src):
            if j >= 1:
                nc.scalar.wait_ge(pl_sd, j)
            nc.scalar.activation(JUNK[:, :], src, ACT.Square, accum_out=SS[:, 44 + j:45 + j]).then_inc(pl_sq, 1)
            nc.scalar.wait_ge(pl_sq, j + 1)
            nc.scalar.activation(SD[:, 44 + j:45 + j], SS[:, 44 + j:45 + j], ACT.Sqrt, bias=EPSC[:, 0:1],
                                 scale=1.0 / D).then_inc(pl_sd, 1)

        def plain_rows(j, rows):
            nc.vector.wait_ge(pl_sd, j + 1)
            dlink(nc.vector.reciprocal(RS[:, 44 + j:45 + j], SD[:, 44 + j:45 + j]))
            nc.vector.scalar_tensor_tensor(out=rows, in0=rows, scalar=RS[:, 44 + j:45 + j], in1=GF[:, :],
                                           op0=ALU.mult, op1=ALU.mult).then_inc(pl_x, 1)

        def residual_act(b, n0, ni, last=True):
            split_hi(b + 1)
            for t in range(NT):
                if t == 7 and last:
                    split_hi(b + 2)
                if t >= 1:
                    norm_hi(ni + t - 1, a_hi(t - 1))
                nc.scalar.wait_ge(acc_dve, freed(n0 + 8 + t)[1])
                norm_stats(ni + t, X[:, t, :])
            norm_hi(ni + 7, a_hi(7))

        def residual_dve(b, n0, ni, gain_count, loaded=None):
            for half in range(2):
                if half == 1:
                    nc.vector.wait_ge(gain_in, gain_count)
                for t in range(NT):
                    if t == 7:
                        split_lo(b + half + 1)
                    n = n0 + 8 * half + t
                    if loaded:
                        nc.vector.wait_ge(loaded[t], 16)
                    nc.vector.wait_ge(acc_ready, n + 1)
                    xs = X[:, t, 512 * half:512 * (half + 1)]
                    nc.vector.tensor_tensor(xs, xs, acc(n), ALU.add).then_inc(acc_dve, 1)
                    if half == 1:
                        if t >= 1:
                            norm_lo(ni + t - 1, a_hi(t - 1), a_lo(t - 1))
                        norm_rows(ni + t, X[:, t, :])
            norm_lo(ni + 7, a_hi(7), a_lo(7))

        def residual_pe(b, n0, ni):
            gemm_tokens(b, n0)
            gemm_tokens(b + 1, n0 + 8, after=lambda t: norm_transpose(ni + t - 1) if t >= 1 else None)
            norm_transpose(ni + 7)

        N_MIX, N_XAT, N_MEM, N_MLP = 0, 8, 16, 18
        N_B2, N_CTX, N_EXP = 26, 34, 36

        ADA_STEPS = 2 * (6 * D // 512)
        ada_in = [sem("ada_in0"), sem("ada_in1")]
        bias_in, mod_made, mod_out = [sem("bias_in0"), sem("bias_in1")], sem("mod_made"), [sem("mod_out0"), sem("mod_out1")]
        ada_acc = sem("ada_acc")
        c_tp, c_silu = sem("c_transposed"), sem("c_silu")
        vt_tp, vt_sb = sem("vectors_transposed"), sem("vectors_ready")
        pad_done = sem("pad_done")
        trig = sem("trig_ready")
        conv_n = sem("conv_ops")
        sg_ready, u_ready = sem("sigmoid_ready"), sem("conv_u_ready")
        ret_in = sem("ret_consts_in")
        ret_tp, ret_q, ret_k, ret_kz = sem("ret_qk_T"), sem("ret_q_split"), sem("ret_k_copied"), sem("ret_kz")
        ret_s, ret_st, ret_y, ret_kv, ret_state = (sem(s) for s in ("ret_s", "ret_masked", "ret_y_sum", "ret_kv_sum", "ret_state_new"))
        ret_d, ret_sq, ret_sd, ret_yn, ret_ty, ret_hi, ret_lo, ret_gw = (
            sem(s) for s in ("ret_d", "ret_sq", "ret_sd", "ret_yn", "ret_ty", "ret_hi", "ret_lo", "ret_gw"))
        ln_mean, ln_d, ln_sq, ln_var, ln_sd, ln_yn, ln_silu, ln_hi, ln_lo = (
            sem("ln_" + s) for s in ("mean", "d", "sq", "var", "sd", "yn", "silu", "hi", "lo"))
        x2_in = [sem(f"x_again{t}") for t in range(NT)]
        mem_in, ctx_in = sem("mem_in"), sem("ctx_in")
        xa_s, xa_m, xa_e, xa_p, xa_t, xa_pt, xa_o, xa_hi, xa_lo = (
            sem("xa_" + s) for s in ("scores", "max", "exp", "probs", "probs_T", "copied", "out", "hi", "lo"))
        u_sq, u_hi, u_lo = sem("hidden_squared"), sem("hidden_hi_made"), sem("hidden_lo_made")
        mod_in, gain_made = sem("mod_rows_in"), sem("gain_made")
        wr_in, gt2_in = sem("router_w_in"), sem("gate_row2_in")
        pl_sq, pl_sd, pl_x = sem("final_sum"), sem("final_rms"), sem("final_rows")
        x_saved = sem("x_saved")
        rt_tp, rt_cp, kz_zero = sem("rot_transposed"), sem("rot_copied"), sem("k_zeroed")
        u2_pad, c2_n, c2_hi, c2_lo = sem("short_conv_pad"), sem("short_conv_ops"), sem("short_conv_hi"), sem("short_conv_lo")
        at_s, at_m, at_e, at_t, at_c, at_o, at_on, at_ot, at_hi, at_lo = (
            sem("wa_" + s) for s in ("scores", "max", "exp", "probs_T", "copied", "out", "normed", "out_T", "hi", "lo"))
        h2_out, x3_out = [sem("h2_out0"), sem("h2_out1")], sem("x3_out")
        x3_new, rt_r, rt_m, rt_e, rt_a, rt_at, rt_ac = (
            sem("router_" + s) for s in ("x", "sum", "max", "exp", "aff", "aff_T", "aff_copied"))
        tk, tk_tp, tk_out = sem("topk"), sem("topk_T"), sem("topk_out")
        ew_in, ew_half = [sem(f"expert_w_in{i}") for i in range(6)], [sem(f"expert_w_half{i}") for i in range(3)]
        xs_in, y_out, y_free = sem("expert_rows_in"), sem("expert_out_stored"), sem("expert_out_free")
        ex_xl = sem("ex_rows_lo")
        W_SPLIT = 4 * (B_W2 + 2)
        ex_xt, ex_xc, ex_g, ex_sg, ex_u, ex_he, ex_ht, ex_hc, ex_d, ex_y, ex_gv = (
            sem("ex_" + s) for s in ("rows_T", "rows_copied", "gate", "silu", "up", "hidden", "hidden_T", "hidden_copied",
                                     "down", "out", "gate_col"))
        fin_out = sem("final_out")

        block = stack.enter_context(nc.Block())

        @block.sync
        def _(sp):
            sp.dma_start(CST[:, :], consts).then_inc(cst_in, 16)
            for t in range(NT):
                sp.dma_start(X[:, t, :], x[0, tok(t), :]).then_inc(x_in[t], 16)
            for half in range(2):
                src, w = w_source(0, half)
                sp_load(0, half, src, w)
            def load_blocks(first, last):
                for b in range(first, last):
                    for half in range(2):
                        src, w = w_source(b, half)
                        sp_load(b, half, src, w)

            load_blocks(1, B_WO)
            for n in range(ADA_STEPS):
                block_, half = n // 2, n % 2
                if n < 2:
                    sp.wait_ge(w_ready, 4 * (B_WO - 1) + 2 * (half + 1))
                else:
                    sp.wait_ge(ada_acc, n - 1)
                sp.dma_start(raw[:, half, :, :], w_ada_2[0, 512 * half:512 * (half + 1), 512 * block_:512 * (block_ + 1)]
                             .rearrange("(k p) n -> p k n", p=P)).then_inc(ada_in[half], 16)
            sp.wait_ge(ada_acc, ADA_STEPS)
            load_blocks(B_WO, B_ML)
            def up_piece(f, half):
                return mlp_up_w[:, bass.ds(f * FB, FB)].rearrange("(k p) n -> p k n", p=P)[:, 4 * half:4 * half + 4, :]

            def down_piece(f, half):
                return mlp_down_w[bass.ds(f * FB + 2 * P * half, 2 * P), :].rearrange("(k p) n -> p k n", p=P)

            def two_rows(half):
                return raw[:, half, :, :].rearrange("p (k a) n -> p k (a n)", a=2)

            for half in range(2):
                sp_load(B_ML, half, mlp_up_w[:, 0:FB].rearrange("(k p) n -> p k n", p=P)[:, 4 * half:4 * half + 4, :])
            with sp.Fori(0, NFB - 1) as f:
                for half in range(2):
                    sp.wait_ge(w_ready, f * 8 + 4 * B_ML + 2 * (half + 1))
                    sp.dma_start(two_rows(half), down_piece(f, half)).then_inc(w_raw[half], 16)
                for half in range(2):
                    sp.wait_ge(w_ready, f * 8 + 4 * (B_ML + 1) + 2 * (half + 1))
                    sp.dma_start(raw[:, half, :, :], up_piece(f + 1, half)).then_inc(w_raw[half], 16)
            for half in range(2):
                sp.wait_ge(w_ready, 4 * (B_I2 - 2) + 2 * (half + 1))
                sp.dma_start(two_rows(half), mlp_down_w[(NFB - 1) * FB + 2 * P * half:(NFB - 1) * FB + 2 * P * (half + 1), :]
                             .rearrange("(k p) n -> p k n", p=P)).then_inc(w_raw[half], 16)
            for b in range(B_I2, B_W2 + 2):
                for half in range(2):
                    src, w = w_source(b, half)
                    sp_load(b, half, src, w)
            mats = (w_gate_2, w_up_2, w_down_2)
            frees = (ew_half[0], ex_g, ew_half[1], ex_u, ew_half[2], ex_d)

            def load_expert(e, m, half, when=None):
                slot = 2 * m + half
                if when is not None:
                    sp.wait_ge(frees[slot], when)
                w = mats[m]
                if isinstance(e, int):
                    src = w[0, e, 512 * half:512 * (half + 1), :]
                else:
                    src = w[0, bass.ds(e, 1), 512 * half:512 * (half + 1), :].rearrange("a k n -> (a k) n")
                sp.dma_start(EW[slot][:, :, :], src.rearrange("(k p) n -> p k n", p=P)).then_inc(ew_in[slot], 16)

            sp.wait_ge(acc_ready, T_W2 + 16)
            for m in range(3):
                for half in range(2):
                    load_expert(0, m, half)
            for m in range(2):
                for half in range(2):
                    load_expert(1, m, half, when=1)
            with sp.Fori(2, NE) as e:
                for m in range(2):
                    for half in range(2):
                        load_expert(e, m, half, when=e)
                for half in range(2):
                    load_expert(e - 1, 2, half, when=e - 1)
            for half in range(2):
                load_expert(NE - 1, 2, half, when=NE - 1)
            sp.wait_ge(fin_out, 16 * NT)

        @block.gpsimd
        def _(pool):
            def row(dst, src, s):
                nc.gpsimd.dma_start(dst, src.partition_broadcast(dst.shape[0])).then_inc(s, 16)

            row(GAIN[:, :], norm_mix_w, gain_in)
            pool.dma_start(C8[0:8, :], c_2[0].rearrange("(k p) -> k p", p=P)).then_inc(vec_in, 16)
            pool.dma_start(C8[8:16, :], c_ctx_2.rearrange("(k p) -> k p", p=P)).then_inc(vec_in, 16)
            pool.dma_start(VEC[0:TAPS, :], conv_w).then_inc(vec_in, 16)
            for n, v in enumerate((conv_b, conv_ln_w, conv_ln_b)):
                pool.dma_start(VEC[TAPS + n:TAPS + n + 1, :], v.rearrange("(a n) -> a n", a=1)).then_inc(vec_in, 16)
            pool.dma_start(VEC[34:37, :], conv_w_2[0]).then_inc(vec_in, 16)
            with nc.allow_non_contiguous_dma(reason="1024 positions"):
                pool.dma_start(POS[:, :], positions[0].rearrange("(t p) -> p t", p=P)).then_inc(vec_in, 16)
            row(SINK[:, :], sink_2[0], vec_in)
            pool.memset(EPSC[:, :], EPS).then_inc(pad_done, 1)
            pool.memset(U[:, :, 0:PADT], 0.0).then_inc(pad_done, 1)
            pool.wait_ge(acc_ready, T_G + 8)
            pool.dma_start(RC[:, :], rconsts).then_inc(ret_in, 16)
            row(GNW[:, :], ret_gn_w, ret_in)
            for j in range(ADA_STEPS // 2 + 2):
                if j >= 2:
                    i = j - 2
                    pool.wait_ge(mod_made, i + 1)
                    pool.dma_start(mod_d[:, 512 * i:512 * (i + 1)], MODB[:, i % 2, :]).then_inc(mod_out[i % 2], 16)
                if j < ADA_STEPS // 2:
                    pool.dma_start(BIAS[:, j % 2, :], b_ada_2[:, 512 * j:512 * (j + 1)]).then_inc(bias_in[j % 2], 16)
            for n in range(2):
                pool.wait_ge(mod_out[n], 16 * (ADA_STEPS // 4))
            pool.wait_ge(ret_lo, 8)
            for t in range(NT):
                pool.dma_start(X[:, t, :], x[0, tok(t), :]).then_inc(x2_in[t], 16)
            pool.wait_ge(ln_yn, 4)
            row(GAIN[:, :], norm_xattn_w, gain_in)
            pool.wait_ge(ln_lo, 4)
            for m in range(2):
                pool.dma_start(MX[:, m, :], mem[0, tok(m), :]).then_inc(mem_in, 16)
            pool.wait_ge(nm_xn, N_MEM)
            row(GAIN[:, :], norm_mem_w, gain_in)
            pool.wait_ge(xa_lo, 16)
            row(GAIN[:, :], norm_mlp_w, gain_in)
            pool.wait_ge(nm_tp, 2 * N_B2)
            row(GAIN[:, :], g_mix_2[0], mod_in)
            row(XN[:, 0, :], mod_d[0, D:2 * D], mod_in)
            row(SHIFT[:, :], mod_d[0, 0:D], mod_in)
            row(GF[:, :], norm_f_w, mod_in)
            pool.wait_ge(acc_ready, T_ML + 24 * NFB)
            pool.dma_start(MX[:, 0, :], ctx_2[0, tok(0), :]).then_inc(ctx_in, 16)
            pool.dma_start(MX[:, 1, :], ctx_2[0, tok(1), :]).then_inc(ctx_in, 16)
            row(GC[:, :], g_mix_2[0], ctx_in)
            row(SHC[:, :], mod_d[1, 0:D], ctx_in)
            for t in range(NT):
                pool.wait_ge(pl_x, t + 1)
                pool.dma_start(xsave_d[tok(t), :], X[:, t, :]).then_inc(x_saved, 16)
            row(RT2[:, :, :].rearrange("p a n -> p (a n)"), mod_d[1, D:2 * D], ctx_in)
            pool.wait_ge(x_saved, 16 * NT)
            pool.wait_ge(nm_xn, N_CTX)
            pool.memset(KZ4[64:128, 0:4:2, :], 0.0).then_inc(kz_zero, 1)
            pool.memset(KZ4[0:64, 1:4:2, :], 0.0).then_inc(kz_zero, 1)
            pool.wait_ge(acc_ready, T_KV + 10)
            pool.memset(U2[:, :, 0:S + 2:S + 1], 0.0).then_inc(u2_pad, 1)
            pool.wait_ge(c2_lo, 4)
            row(GT1[:, :], mod_d[0, 2 * D:3 * D], mod_in)
            row(SCT[:, :], mod_d[0, 4 * D:5 * D], mod_in)
            pool.wait_ge(at_lo, 8)
            row(GAIN[:, :], g_ffn_2[0], mod_in)
            row(SHIFT[:, :], mod_d[0, 3 * D:4 * D], mod_in)
            for t in range(NT):
                pool.dma_start(X[:, t, :], xsave_d[tok(t), :]).then_inc(x2_in[t], 16)
            pool.dma_start(WR[:, :, :], w_router_2[0].rearrange("(k p) n -> p k n", p=P)).then_inc(wr_in, 16)
            for t in range(NT):
                pool.wait_ge(x3_new, t + 1)
                pool.dma_start(acc_d[tok(t), :], X[:, t, :]).then_inc(x3_out, 16)
                pool.wait_ge(nm_xn, N_EXP + t + 1)
                pool.dma_start(h2_d[tok(t), :], XN[:, t % 2, :]).then_inc(h2_out[t % 2], 16)
            row(GT2[:, :], mod_d[0, 5 * D:6 * D], gt2_in)
            pool.wait_ge(x3_out, 16 * NT)
            for n in range(2):
                pool.wait_ge(h2_out[n], 16 * (NT // 2))
            pool.wait_ge(tk_out, 1)
            row(GF[:, :], g_final_2, gain_in)
            pool.sem_inc(y_free, 1)

            def gather(e):
                pool.indirect_dma_start(XS[:, :], None, h2_d[:, :], bass.IndirectOffsetOnAxis(ap=GI[:, e:e + 1], axis=0)).then_inc(xs_in, 16)

            gather(0)
            for e in range(-2, NE):
                if e < NE - 3:
                    pool.wait_ge(ex_xt, e + 3)
                    gather(e + 3)
                if e < 0:
                    continue
                pool.wait_ge(ex_y, e + 2)
                pool.indirect_dma_start(acc_d[:, :], bass.IndirectOffsetOnAxis(ap=GI[:, e:e + 1], axis=0), YE[:, :], None,
                                        compute_op=ALU.add).then_inc(y_out, 16)
                pool.wait_ge(y_out, 16 * e + 16)
                pool.sem_inc(y_free, 1)
            for t in range(NT):
                pool.dma_start(X[:, t, :], acc_d[tok(t), :]).then_inc(x2_in[t], 16)
            for t in range(NT):
                pool.wait_ge(pl_x, 8 + t + 1)
                pool.dma_start(out[0, tok(t), :], X[:, t, :]).then_inc(fin_out, 16)
            pool.wait_ge(fin_out, 16 * NT)

        @block.scalar
        def _(act):
            act.wait_ge(pad_done, 1)
            for t in range(NT):
                act.wait_ge(x_in[t], 16)
                norm_stats(N_MIX + t, X[:, t, :])
                if t >= 1:
                    norm_hi(N_MIX + t - 1, a_hi(t - 1))
            norm_hi(N_MIX + 7, a_hi(7))
            act.wait_ge(c_tp, 1)
            act.activation(CS[:, :, :], BK[0][:, 0:16].rearrange("p (a k) -> p a k", a=2), ACT.Silu).then_inc(c_silu, 1)
            split_hi(0)
            act.wait_ge(trig, 1)
            act.activation(CS1[:, :, :, :], ANK[:, :, :, :], ACT.Sin).then_inc(trig, 1)
            for m in range(8):
                if m == 7:
                    split_hi(1)
                act.wait_ge(acc_ready, T_CB + m + 1)
                h, c = m // 4, m % 4
                act.activation(YC[:, c, h * 512:(h + 1) * 512], acc(T_CB + m)[:, :], ACT.Sigmoid).then_inc(acc_act, 1)
            split_hi(2)
            split_hi(3)
            for t in range(NT):
                if t == 7:
                    split_hi(4)
                act.wait_ge(acc_ready, T_V + t + 1)
                act.activation(V[:, t, :], acc(T_V + t)[:, :], ACT.Copy).then_inc(acc_act, 1)
            for t in range(NT):
                act.wait_ge(acc_ready, T_G + t + 1)
                act.activation(G[:, t, :], acc(T_G + t)[:, :], ACT.Silu).then_inc(acc_act, 1)
            for t in range(NT):
                act.wait_ge(ret_tp, t + 1)
                if t >= 1:
                    act.wait_ge(ret_s, t)
                act.activation(KTT[:, :, :], BK[4][:, 256:512].rearrange("p (g n) -> p g n", g=2), ACT.Copy).then_inc(ret_k, 1)
                act.wait_ge(ret_d, t + 1)
                act.activation(YSQ[:, :], YD[:, :], ACT.Square).then_inc(ret_sq, 1)
                act.wait_ge(ret_yn, 2 * t + 1)
                act.activation(YST[:, 2, :], YST[:, 1, :], ACT.Sqrt, bias=EPSC[:, 0:1], scale=1.0 / DV).then_inc(ret_sd, 1)
                for j in range(ADA_STEPS // 2):
                    if 3 * t < 2 * j + 2 <= 3 * t + 3:
                        act.wait_ge(ada_acc, 2 * j + 2)
                        if j >= 2:
                            act.wait_ge(mod_out[j % 2], 16 * (j // 2))
                        act.activation(MODB[:, j % 2, :], BK[2 + j % 2][0:2, :], ACT.Copy).then_inc(mod_made, 1)
                act.wait_ge(ret_ty, t + 1)
                act.activation(AH[:, 4:8, tok(t)], BK[1][:, :].rearrange("p (c n) -> p c n", c=4), ACT.Copy).then_inc(ret_hi, 1)
            split_hi(B_WO)
            act.wait_ge(ln_d, 8)
            for c in range(4):
                act.activation(SQ[:, c, :], YC[:, c, :], ACT.Square).then_inc(ln_sq, 1)
            for h in range(2):
                act.wait_ge(ln_var, h + 1)
                act.activation(SDL[:, h * 512:(h + 1) * 512], BK[2 + h][:, :], ACT.Sqrt, bias=EPSC[:, 0:1]).then_inc(ln_sd, 1)
            for n in range(2):
                act.wait_ge(mod_out[n], 16 * (ADA_STEPS // 4))
            for c in range(4):
                act.wait_ge(ln_yn, c + 1)
                act.activation(SQ[:, c, :], YC[:, c, :], ACT.Silu, scale=VT[:, c, 32:33], bias=VT[:, c, 33:34]).then_inc(ln_silu, 1)
                act.wait_ge(ln_silu, c + 1)
                act.activation(AH[:, c, :], SQ[:, c, :], ACT.Copy).then_inc(ln_hi, 1)
            residual_act(B_WO, T_WO, N_XAT)
            act.wait_ge(mem_in, 32)
            for m in range(2):
                norm_stats(N_MEM + m, MX[:, m, :])
            for m in range(2):
                norm_hi(N_MEM + m, MTH[:, :, tok(m)])
            for kb in range(2):
                for c in range(4):
                    if c == 3:
                        split_hi(B_KV + kb + 1)
                    n = T_MK + 4 * kb + c
                    act.wait_ge(acc_ready, n + 1)
                    act.activation(KX[:, 4 * kb + c, :], acc(n)[:, 0:MEM], ACT.Copy).then_inc(acc_act, 1)
            for vb in range(2):
                for m in range(2):
                    if m == 1:
                        split_hi(B_KV + vb + 3)
                    n = T_MV + 2 * vb + m
                    act.wait_ge(acc_ready, n + 1)
                    act.activation(VX[:, m, 512 * vb:512 * (vb + 1)], acc(n), ACT.Copy).then_inc(acc_act, 1)
            for qb in range(2):
                for m in range(8):
                    if m == 7:
                        split_hi(B_XQ + qb + 1)
                    n = T_XQ + 8 * qb + m
                    h, c = m // 4, m % 4
                    act.wait_ge(acc_ready, n + 1)
                    act.activation(QT[:, 4 * qb + c, h * 512:(h + 1) * 512], acc(n), ACT.Copy).then_inc(acc_act, 1)
            for u in range(16 + 2):
                if u < 16:
                    act.wait_ge(xa_m, u + 1)
                    if u >= 2:
                        act.wait_ge(xa_t, u - 1)
                    for h in range(2):
                        i_ = act.activation(PX[:, u % 2, 256 * h:256 * (h + 1)], BK[4 + u % 2][:, 256 * h:256 * (h + 1)], ACT.Exp,
                                            bias=XM[:, u, h:h + 1], scale=XD ** -0.5, accum_out=XL[:, u, h:h + 1])
                    i_.then_inc(xa_e, 1)
                if 1 <= u <= 16:
                    w = u - 1
                    act.wait_ge(xa_t, w + 1)
                    if w >= 2:
                        act.wait_ge(xa_o, w - 1)
                    act.activation(PT[:, w % 2, :, :], BK[6 + w % 2].rearrange("p (c n) -> p c n", c=4), ACT.Copy).then_inc(xa_pt, 1)
                if u >= 2:
                    w = u - 2
                    t, hp = w // 2, w % 2
                    act.wait_ge(xa_o, w + 1)
                    act.activation(AH[:, 4 * hp:4 * hp + 4, tok(t)], BK[w % 4].rearrange("p (c n) -> p c n", c=4),
                                   ACT.Copy).then_inc(xa_hi, 1)
            residual_act(B_XO, T_XO, N_MLP)
            def hidden_hi(m, f):
                h, c = m // 4, m % 4
                act.wait_ge(u_sq, f * 8 + m + 1)
                act.activation(UH[:, c, h * 512:(h + 1) * 512], UF[:, m % 2, :], ACT.Copy).then_inc(u_hi, 1)

            def mlp_block(f):
                for m in range(8):
                    if m == 7:
                        split_hi(B_ML + 1, off=2 * f)
                    act.wait_ge(acc_ready, f * 24 + T_ML + m + 1)
                    act.wait_ge(u_lo, f * 8 + m + 1)
                    act.activation(UF[:, m % 2, :], acc(T_ML + m), ACT.Relu).then_inc(acc_act, 1)
                    if m >= 1:
                        hidden_hi(m - 1, f)
                hidden_hi(7, f)

            with act.Fori(0, NFB - 1) as f:
                mlp_block(f)
                split_hi(B_ML + 2, off=2 * f)
            mlp_block(NFB - 1)
            act.wait_ge(gain_made, 1)
            for t in range(NT + 2):
                if t < NT:
                    if t == NT - 1:
                        split_hi(B_I2)
                    act.wait_ge(acc_dve, freed(T_ML + 24 * (NFB - 1) + 8 + 2 * t + 1)[1])
                    plain_stats(t, X[:, t, :])
                if 1 <= t <= NT:
                    act.wait_ge(pl_x, t)
                    norm_stats(N_B2 + t - 1, X[:, t - 1, :])
                if t >= 2:
                    norm_hi(N_B2 + t - 2, a_hi(t - 2))
            act.wait_ge(ctx_in, 16 * 5)
            norm_stats(N_CTX, MX[:, 0, :])
            norm_stats(N_CTX + 1, MX[:, 1, :])
            norm_hi(N_CTX, MTH[:, :, tok(0)])
            norm_hi(N_CTX + 1, MTH[:, :, tok(1)])

            def rot_copy(r):
                act.wait_ge(rt_tp, r + 1)
                ps = BK[4 + r % 4]
                if r < 8:
                    act.activation(QT2[:, :, tok(r)], ps.rearrange("p (c n) -> p c n", c=4), ACT.Copy).then_inc(rt_cp, 1)
                    return
                act.wait_ge(kz_zero, 2)
                i_ = tok(r - 8)
                act.activation(KZ4[0:64, 0, i_], ps[0:64, 0:P], ACT.Copy)
                act.activation(KZ4[0:64, 2, i_], ps[0:64, P:2 * P], ACT.Copy)
                act.activation(KZ4[64:128, 3, i_], ps[64:128, 0:P], ACT.Copy)
                act.activation(KZ4[64:128, 1, i_], ps[64:128, P:2 * P], ACT.Copy).then_inc(rt_cp, 1)

            for r in range(18):
                if r == 7:
                    split_hi(B_I2 + 1)
                if r == 17:
                    split_hi(B_I2 + 2)
                if r >= 1:
                    rot_copy(r - 1)
            rot_copy(17)
            for m in range(8):
                if m == 0:
                    act.wait_ge(u2_pad, 1)
                if m == 7:
                    split_hi(B_I2 + 3)
                h, c = m // 4, m % 4
                act.wait_ge(acc_ready, T_CG + m + 1)
                act.activation(U2[:, c, 1 + h * 512:1 + (h + 1) * 512], acc(T_CG + m), ACT.Copy).then_inc(acc_act, 1)
            split_hi(B_I2 + 4)
            split_hi(B_W2)
            act.wait_ge(acc_dve, freed(T_BG + 7)[1])
            for c in range(4):
                act.activation(AH[:, 4 + c, :], C2[:, c, :], ACT.Copy).then_inc(c2_hi, 1)
            for v in range(64 + 7):
                if v < 64:
                    t, h = v // 8, v % 8
                    w = 640 if 0 < t < 7 else 512
                    act.wait_ge(at_m, v + 1)
                    if v >= 2:
                        act.wait_ge(at_t, v - 1)
                    act.activation(P2[:, v % 2, 0:w], PAIR[v % 2][:, 0:w], ACT.Exp, bias=NM2[:, v:v + 1], scale=AD ** -0.5,
                                   accum_out=L2[:, v:v + 1])
                    act.activation(ES2[:, v:v + 1], NM2[:, v:v + 1], ACT.Exp, bias=SINK[:, h:h + 1]).then_inc(at_e, 1)
                if v >= 6 and (v - 6) % 8 == 7:
                    t = (v - 6) // 8
                    act.wait_ge(at_ot, t + 1)
                    act.activation(AH[:, 0:4, tok(t)], BK[6 + t % 2].rearrange("p (c n) -> p c n", c=4), ACT.Copy).then_inc(at_hi, 1)
            split_hi(B_W2 + 1)

            def router_exp(t):
                act.wait_ge(rt_m, t + 1)
                act.activation(REX[:, t % 2, :], BK[6 + t % 2][:, 0:NE], ACT.Exp, bias=RST[:, 0, t:t + 1],
                               accum_out=RST[:, 1, t:t + 1]).then_inc(rt_e, 1)

            def router_copy(t):
                act.wait_ge(rt_at, t + 1)
                act.activation(AFT[:, tok(t)], BK[6 + t % 2][0:NE, P:2 * P], ACT.Copy).then_inc(rt_ac, 1)

            def h2_copy(t):
                for hb in range(2):
                    q = 2 * (N_EXP + t) + hb
                    act.wait_ge(nm_tp, q + 1)
                    if t >= 2 and hb == 0:
                        act.wait_ge(rt_r, t - 1)
                    act.activation(HTR[:, t % 2, 4 * hb:4 * hb + 4, :], BK[4 + q % 2].rearrange("p (c n) -> p c n", c=4),
                                   ACT.Copy).then_inc(nm_hi, 1)

            for t in range(NT + 4):
                if 1 <= t <= NT:
                    h2_copy(t - 1)
                if t < NT:
                    act.wait_ge(x3_new, t + 1)
                    if t >= 2:
                        act.wait_ge(h2_out[t % 2], 16 * (t // 2))
                    elif t == 0:
                        act.wait_ge(gain_made, 3)
                    norm_stats(N_EXP + t, X[:, t, :])
                if 2 <= t < NT + 2:
                    router_exp(t - 2)
                if 3 <= t < NT + 3:
                    router_copy(t - 3)
            def expert_w_hi(slot, e):
                act.wait_ge(ew_in[slot], 16 * e + 16)
                for j in range(2):
                    act.activation(EWH[slot][:, 2 * j:2 * j + 2, :], EW[slot][:, 2 * j:2 * j + 2, :], ACT.Copy).then_inc(w_hi, 1)

            def expert_rows_hi(e):
                act.wait_ge(ex_xt, e + 1)
                act.activation(XTH[:, :, :], PAIR[3][:, :].rearrange("p (c n) -> p c n", c=8), ACT.Copy).then_inc(ex_xc, 1)

            expert_w_hi(0, 0)
            for n in range(2):
                act.wait_ge(h2_out[n], 16 * (NT // 2))
            expert_w_hi(1, 0)
            act.wait_ge(x3_out, 16 * NT)
            expert_w_hi(2, 0)
            act.wait_ge(tk_out, 1)
            expert_w_hi(3, 0)
            expert_rows_hi(0)

            def expert_act(e, more=True, first=False):
                act.wait_ge(ex_g, e + 1)
                if not first:
                    act.wait_ge(ex_he, e)
                act.activation(SG[:, :], PAIR[0][:, :], ACT.Silu).then_inc(ex_sg, 1)
                if more:
                    expert_w_hi(0, e + 1)
                    expert_w_hi(1, e + 1)
                    expert_rows_hi(e + 1)
                    expert_w_hi(2, e + 1)
                    expert_w_hi(3, e + 1)
                act.wait_ge(ex_ht, e + 1)
                act.activation(HTE[:, :, :], PAIR[3][:, :].rearrange("p (c n) -> p c n", c=8), ACT.Copy).then_inc(ex_hc, 1)

            expert_act(0, first=True)
            with act.Fori(1, NE - 1) as e:
                expert_act(e)
            expert_act(NE - 1, more=False)
            for t in range(NT):
                act.wait_ge(x2_in[t], 48)
                plain_stats(8 + t, X[:, t, :])

        @block.vector
        def _(dve):
            dve.wait_ge(cst_in, 16)
            dve.wait_ge(gain_in, 16)
            for t in range(NT):
                norm_rows(N_MIX + t, X[:, t, :])
                if t >= 1:
                    norm_lo(N_MIX + t - 1, a_hi(t - 1), a_lo(t - 1))
            norm_lo(N_MIX + 7, a_hi(7), a_lo(7))
            split_lo(0)
            dve.wait_ge(vec_in, 16 * 9)
            dve.wait_ge(vt_tp, 1)
            dve.tensor_copy(VT[:, :, :], BK[1][:, 0:148].rearrange("p (c r) -> p c r", c=4)).then_inc(vt_sb, 1)
            dve.tensor_scalar(NSINK[:, :], SINK[:, :], -1.0, None, ALU.mult)
            dve.tensor_copy(IDB[:, :], IDN)
            dve.tensor_copy(MKB[:, :, :], CST[:, CM:CM + 2 * P].rearrange("p (a n) -> p a n", a=2)).then_inc(vt_sb, 1)
            dlink(dve.tensor_copy(POSF[:, :], POS[:, :]))
            dlink(dve.tensor_tensor(ANG[:, :, :], POSF[:, :].unsqueeze(2).to_broadcast([P, NT, 16]),
                                    CST[:, CF:CF + 16].unsqueeze(1).to_broadcast([P, NT, 16]), ALU.mult))
            TWO_PI = 2 * np.pi
            c1 = 6.28125
            c2 = float(np.round((TWO_PI - c1) * 2 ** 18) / 2 ** 18)
            c3 = float(TWO_PI - c1 - c2)
            for n, (turn, back) in enumerate(((0.25, np.pi / 2), (0.0, 0.0))):
                a = ANK[:, n, :, :]
                kk = RT[:, n, 0:128].rearrange("p (t f) -> p t f", t=NT)
                dlink(dve.tensor_scalar(kk, ANG[:, :, :], float(1 / TWO_PI), float(turn), ALU.mult, ALU.add))
                dlink(dve.tensor_scalar(kk, kk, MAGIC, None, ALU.add))
                dlink(dve.tensor_scalar(kk, kk, MAGIC, None, ALU.subtract))
                dlink(dve.scalar_tensor_tensor(out=a, in0=kk, scalar=-c1, in1=ANG[:, :, :], op0=ALU.mult, op1=ALU.add))
                dlink(dve.scalar_tensor_tensor(out=a, in0=kk, scalar=-c2, in1=a, op0=ALU.mult, op1=ALU.add))
                dlink(dve.scalar_tensor_tensor(out=a, in0=kk, scalar=-c3, in1=a, op0=ALU.mult, op1=ALU.add))
                dlink(dve.tensor_scalar(a, a, float(back), None, ALU.add))
                dlink(dve.tensor_scalar(kk, a, float(1 / TWO_PI), MAGIC, ALU.mult, ALU.add))
                dlink(dve.tensor_scalar(kk, kk, MAGIC, None, ALU.subtract))
                dlink(dve.scalar_tensor_tensor(out=a, in0=kk, scalar=-TWO_PI, in1=a, op0=ALU.mult, op1=ALU.add))
                dlink(dve.tensor_scalar(a, a, 3.1415925, None, ALU.min))
                dlink(dve.tensor_scalar(a, a, -3.1415925, None, ALU.max))
            dve.tensor_copy(POSF[:, 0:1], POS[:, 0:1]).then_inc(trig, 1)
            dve.wait_ge(trig, 2)
            dve.wait_ge(pad_done, 2)
            for m in range(8):
                if m == 7:
                    split_lo(2)
                if m == 0:
                    split_lo(1)
                h, c = m // 4, m % 4
                dve.wait_ge(acc_act, freed(T_CB + m)[1])
                dve.wait_ge(acc_ready, T_CA + m + 1)
                dve.tensor_tensor(U[:, c, PADT + h * 512:PADT + (h + 1) * 512], acc(T_CA + m)[:, :],
                                  YC[:, c, h * 512:(h + 1) * 512], ALU.mult).then_inc(acc_dve, 1)
            dve.wait_ge(acc_dve, freed(T_CA + 7)[1])

            def conv_tap(j):
                for c in range(4):
                    src = U[:, c, j:j + S]
                    w = VT[:, c, j:j + 1]
                    if j == 0:
                        i_ = dve.tensor_scalar(YC[:, c, :], src, w, VT[:, c, 31:32], ALU.mult, ALU.add)
                    else:
                        dve.wait_ge(conv_n, 4 * (j - 1) + c + 1)
                        i_ = dve.scalar_tensor_tensor(out=YC[:, c, :], in0=src, scalar=w, in1=YC[:, c, :],
                                                      op0=ALU.mult, op1=ALU.add)
                    i_.then_inc(conv_n, 1)

            for t in range(NT):
                if t == 7:
                    split_lo(3)
                dve.wait_ge(acc_ready, T_QK + t + 1)
                ps = acc(T_QK + t)[:, :].rearrange("p (h a f) -> p h a f", a=2, f=16)
                co = CS1[:, 0, t, :].unsqueeze(1).to_broadcast([P, 16, 16])
                si = CS1[:, 1, t, :].unsqueeze(1).to_broadcast([P, 16, 16])
                tmp = [RT[:, n, :].rearrange("p (h f) -> p h f", f=16) for n in range(4)]
                if t >= 1:
                    dve.wait_ge(acc_dve, freed(T_QK + t - 1)[1])
                dve.tensor_tensor(tmp[0], ps[:, :, 0, :], co, ALU.mult)
                dve.tensor_tensor(tmp[1], ps[:, :, 1, :], si, ALU.mult)
                dve.tensor_tensor(tmp[2], ps[:, :, 0, :], si, ALU.mult)
                dlink(dve.tensor_tensor(tmp[3], ps[:, :, 1, :], co, ALU.mult))
                q = QK[:, t, :].rearrange("p (h a f) -> p h a f", a=2, f=16)
                dve.tensor_tensor(q[:, :, 0, :], tmp[0], tmp[1], ALU.subtract)
                dve.tensor_tensor(q[:, :, 1, :], tmp[2], tmp[3], ALU.add).then_inc(acc_dve, 1)
                if t % 2 == 1 and t // 2 < TAPS_QK:
                    conv_tap(t // 2)
            for j in range(TAPS_QK, TAPS_VG):
                if j == TAPS_QK + 8:
                    split_lo(4)
                conv_tap(j)
            dve.memset(STATE[:, :, :], 0.0).then_inc(ret_state, 1)
            dve.wait_ge(ret_in, 32)
            BQ = RC[:, RQ:RQ + 4].unsqueeze(2).to_broadcast([P, 4, P])

            def ret_a(t):
                dve.wait_ge(ret_k, t + 1)
                if t >= 1:
                    dve.wait_ge(ret_y, t)
                    dve.wait_ge(ret_kv, t)
                for g in range(2):
                    q = BK[4][:, g * P:(g + 1) * P]
                    dve.tensor_tensor(QBD[:, g, :, :], q.unsqueeze(1).to_broadcast([P, 4, P]), BQ, ALU.mult)
                dve.tensor_tensor(QX[:, :, :], BK[4][:, 0:256].rearrange("p (g n) -> p g n", g=2),
                                  RC[:, RX:RX + 256].rearrange("p (g n) -> p g n", g=2), ALU.mult)
                dve.tensor_tensor(KZ[:, :].rearrange("p (h f) -> p h f", f=DK),
                                  QK[:, t, 256:512].rearrange("p (h f) -> p h f", f=DK),
                                  RC[:, RZ:RZ + 8].unsqueeze(2).to_broadcast([P, 8, DK]), ALU.mult).then_inc(ret_q, 1)
                for g in range(2):
                    dve.wait_ge(ret_s, t + 1)
                    i_ = dve.tensor_tensor(ST[:, 4 * g:4 * g + 4, :], BK[5 + g][:, :].rearrange("p (h n) -> p h n", h=4),
                                           RC[:, RM + 512 * g:RM + 512 * (g + 1)].rearrange("p (h n) -> p h n", h=4), ALU.mult)
                i_.then_inc(ret_st, 1)

            def ret_b(t):
                dve.wait_ge(ret_y, t + 1)
                dve.wait_ge(ret_kv, t + 1)
                dlink(dve.tensor_tensor(TKV[:, :, :], BK[0][:, :].rearrange("p (g n) -> p g n", g=2),
                                        RC[:, RB:RB + 512].rearrange("p (g n) -> p g n", g=2), ALU.mult))
                for g in range(2):
                    i_ = dve.scalar_tensor_tensor(out=STATE[:, g, :], in0=STATE[:, g, :], scalar=RC[:, RG + g:RG + g + 1],
                                                  in1=TKV[:, g, :], op0=ALU.mult, op1=ALU.add)
                i_.then_inc(ret_state, 1)
                y = BK[7][:, :].rearrange("p (h f) -> p h f", f=DV)
                dlink(dve.tensor_reduce(YST[:, 0, :], y, AX, ALU.add))
                dlink(dve.tensor_scalar(YST[:, 0, :], YST[:, 0, :], 1.0 / DV, None, ALU.mult))
                if t >= 1:
                    dve.wait_ge(ret_ty, t)
                yd = YD[:, :].rearrange("p (h f) -> p h f", f=DV)
                dve.tensor_tensor(yd, y, YST[:, 0, :].unsqueeze(2).to_broadcast([P, 8, DV]), ALU.subtract).then_inc(ret_d, 1)
                dve.wait_ge(ret_sq, t + 1)
                dve.tensor_reduce(YST[:, 1, :], YSQ[:, :].rearrange("p (h f) -> p h f", f=DV), AX, ALU.add).then_inc(ret_yn, 1)
                dve.wait_ge(ret_sd, t + 1)
                dlink(dve.reciprocal(YST[:, 3, :], YST[:, 2, :]))
                dlink(dve.tensor_tensor(yd, yd, YST[:, 3, :].unsqueeze(2).to_broadcast([P, 8, DV]), ALU.mult))
                dlink(dve.tensor_tensor(YD[:, :], YD[:, :], G[:, t, :], ALU.mult))
                dve.tensor_tensor(YD[:, :], YD[:, :], GNW[:, :], ALU.mult).then_inc(ret_yn, 1)

            def ret_c(t):
                dve.wait_ge(ret_hi, t + 1)
                dve.tensor_tensor(AL[:, 4:8, tok(t)], BK[1][:, :].rearrange("p (c n) -> p c n", c=4),
                                  AH[:, 4:8, tok(t)], ALU.subtract).then_inc(ret_lo, 1)

            for t in range(NT):
                dve.wait_ge(acc_act, freed(T_G + t)[1])
                ret_a(t)
                if TAPS_VG + 2 * t < TAPS:
                    conv_tap(TAPS_VG + 2 * t)
                ret_b(t)
                if TAPS_VG + 1 + 2 * t < TAPS:
                    conv_tap(TAPS_VG + 1 + 2 * t)
                ret_c(t)
            for h in range(2):
                dve.wait_ge(ln_mean, h + 1)
                for c in range(4):
                    y = YC[:, c, h * 512:(h + 1) * 512]
                    dve.tensor_tensor(y, y, BK[2 + h][:, :], ALU.subtract).then_inc(ln_d, 1)
            split_lo(B_WO)
            for h in range(2):
                dve.wait_ge(ln_sd, h + 1)
                i_ = dve.reciprocal(SDL[:, h * 512:(h + 1) * 512], SDL[:, h * 512:(h + 1) * 512])
            dlink(i_)
            dve.wait_ge(ln_d, 8)
            for c in range(4):
                dve.tensor_tensor(YC[:, c, :], YC[:, c, :], SDL[:, :], ALU.mult).then_inc(ln_yn, 1)
            for c in range(4):
                dve.wait_ge(ln_hi, c + 1)
                dve.tensor_tensor(AL[:, c, :], SQ[:, c, :], AH[:, c, :], ALU.subtract).then_inc(ln_lo, 1)
            residual_dve(B_WO, T_WO, N_XAT, 32, x2_in)
            dve.wait_ge(gain_in, 48)
            for m in range(2):
                norm_rows(N_MEM + m, MX[:, m, :])
            for m in range(2):
                norm_lo(N_MEM + m, MTH[:, :, tok(m)], MTL[:, :, tok(m)])
            for b in range(B_KV + 1, B_XO + 1):
                split_lo(b)
            for u in range(16 + 3):
                if u < 16:
                    dve.wait_ge(xa_s, u + 1)
                    ps = BK[4 + u % 2].rearrange("p (h n) -> p h n", h=2)
                    dlink(dve.tensor_reduce(XM[:, u, :], ps, AX, ALU.max))
                    dve.tensor_scalar(XM[:, u, :], XM[:, u, :], -XD ** -0.5, None, ALU.mult).then_inc(xa_m, 1)
                if u >= 3:
                    w = u - 3
                    t, hp = w // 2, w % 2
                    dve.wait_ge(xa_hi, w + 1)
                    dve.tensor_tensor(AL[:, 4 * hp:4 * hp + 4, tok(t)], BK[w % 4].rearrange("p (c n) -> p c n", c=4),
                                      AH[:, 4 * hp:4 * hp + 4, tok(t)], ALU.subtract).then_inc(xa_lo, 1)
                if u < 16:
                    dve.wait_ge(xa_e, u + 1)
                    dlink(dve.reciprocal(XL[:, u, :], XL[:, u, :]))
                    for h in range(2):
                        pr = PX[:, u % 2, 256 * h:256 * (h + 1)]
                        i_ = dve.tensor_scalar(pr, pr, XL[:, u, h:h + 1], None, ALU.mult)
                    i_.then_inc(xa_p, 1)
            residual_dve(B_XO, T_XO, N_MLP, 64)

            def hidden_lo(m, f):
                h, c = m // 4, m % 4
                dve.wait_ge(u_hi, f * 8 + m + 1)
                dve.tensor_tensor(UL[:, c, h * 512:(h + 1) * 512], UF[:, m % 2, :], UH[:, c, h * 512:(h + 1) * 512],
                                  ALU.subtract).then_inc(u_lo, 1)

            def mlp_block(f, after=None):
                for m in range(8):
                    if m == 7:
                        split_lo(B_ML + 1, off=2 * f)
                    dve.wait_ge(acc_act, f * 8 + freed(T_ML + m)[1])
                    dve.tensor_tensor(UF[:, m % 2, :], UF[:, m % 2, :], UF[:, m % 2, :], ALU.mult).then_inc(u_sq, 1)
                    if m >= 1:
                        hidden_lo(m - 1, f)
                hidden_lo(7, f)
                for q in range(16):
                    if q == 15:
                        split_lo(B_ML + 2, off=2 * f)
                    n = T_ML + 8 + q
                    dve.wait_ge(acc_ready, f * 24 + n + 1)
                    xs = X[:, q // 2, 512 * (q % 2):512 * (q % 2 + 1)]
                    dve.tensor_tensor(xs, xs, acc(n), ALU.add).then_inc(acc_dve, 1)
                    if after is not None and q % 2 == 1:
                        after(q // 2)

            def two_norms(t):
                if 1 <= t <= NT:
                    plain_rows(t - 1, X[:, t - 1, :])
                if 2 <= t <= NT + 1:
                    norm_rows(N_B2 + t - 2, X[:, t - 2, :], shift=SHIFT)
                if 3 <= t <= NT + 2:
                    norm_lo(N_B2 + t - 3, a_hi(t - 3), a_lo(t - 3))

            dve.sem_inc(u_lo, 2)
            with dve.Fori(0, NFB - 1) as f:
                mlp_block(f)
            dve.wait_ge(mod_in, 64)
            dve.scalar_tensor_tensor(out=GAIN[:, :], in0=XN[:, 0, :], scalar=1.0, in1=GAIN[:, :], op0=ALU.add,
                                     op1=ALU.mult).then_inc(gain_made, 1)
            dve.wait_ge(gain_made, 1)
            mlp_block(NFB - 1, after=two_norms)
            for t in range(NT, NT + 3):
                two_norms(t)
            dve.wait_ge(ctx_in, 16 * 5)
            dve.scalar_tensor_tensor(out=GC[:, :], in0=RT2[:, :, :].rearrange("p a n -> p (a n)"), scalar=1.0, in1=GC[:, :],
                                     op0=ALU.add, op1=ALU.mult).then_inc(gain_made, 1)
            dve.wait_ge(gain_made, 2)
            norm_rows(N_CTX, MX[:, 0, :], shift=SHC, gain=GC)
            norm_rows(N_CTX + 1, MX[:, 1, :], shift=SHC, gain=GC)
            norm_lo(N_CTX, MTH[:, :, tok(0)], MTL[:, :, tok(0)])
            norm_lo(N_CTX + 1, MTH[:, :, tok(1)], MTL[:, :, tok(1)])

            def rotate(src, dst, heads, t):
                co = COS2[:, t, :].unsqueeze(1).to_broadcast([P, heads, 32])
                si = SIN2[:, t, :].unsqueeze(1).to_broadcast([P, heads, 32])
                tmp = [RT2[:, n, 0:heads * 32].rearrange("p (h f) -> p h f", f=32) for n in range(4)]
                dve.tensor_tensor(tmp[0], src[:, :, 0, :], co, ALU.mult)
                dve.tensor_tensor(tmp[1], src[:, :, 1, :], si, ALU.mult)
                dve.tensor_tensor(tmp[2], src[:, :, 0, :], si, ALU.mult)
                dlink(dve.tensor_tensor(tmp[3], src[:, :, 1, :], co, ALU.mult))
                dve.tensor_tensor(dst[:, :, 0, :], tmp[0], tmp[1], ALU.subtract)
                return dve.tensor_tensor(dst[:, :, 1, :], tmp[2], tmp[3], ALU.add)

            for r in range(18):
                n = (T_Q2 if r < 8 else T_KV - 8) + r
                if r == 7:
                    split_lo(B_I2 + 1)
                if r == 17:
                    split_lo(B_I2 + 2)
                dve.wait_ge(acc_ready, n + 1)
                if r >= 2:
                    dve.wait_ge(rt_tp, r - 1)
                if r >= 1:
                    dve.wait_ge(acc_dve, freed(n)[1] - 1)
                q = QR[:, r % 2, :]
                if r < 8:
                    rotate(acc(n).rearrange("p (h a f) -> p h a f", a=2, f=32), q.rearrange("p (h a f) -> p h a f", a=2, f=32),
                           8, r).then_inc(acc_dve, 1)
                    continue
                if r == 8:
                    dve.wait_ge(kz_zero, 2)
                dve.tensor_copy(V2[:, r - 8, :], acc(n)[:, P:2 * P])
                if r < 10:
                    dlink(dve.tensor_copy(q[:, 0:P], acc(n)[:, 0:P]))
                else:
                    dlink(rotate(acc(n)[:, 0:P].rearrange("p (h a f) -> p h a f", a=2, f=32),
                                 q[:, 0:P].rearrange("p (h a f) -> p h a f", a=2, f=32), 2, r - 10))
                dve.tensor_copy(q[:, P + 64:2 * P], q[:, 0:64])
                dve.tensor_copy(q[:, P:P + 64], q[:, 64:P]).then_inc(acc_dve, 1)
            for m in range(8):
                if m == 0:
                    split_lo(B_I2 + 3)
                if m == 7:
                    split_lo(B_I2 + 4)
                h, c = m // 4, m % 4
                us = U2[:, c, 1 + h * 512:1 + (h + 1) * 512]
                dve.wait_ge(acc_act, freed(T_CG + m)[1])
                dve.wait_ge(acc_ready, T_HV + m + 1)
                dve.tensor_tensor(us, us, acc(T_HV + m), ALU.mult).then_inc(acc_dve, 1)
            dve.wait_ge(acc_dve, freed(T_HV + 7)[1])
            for j in range(3):
                for c in range(4):
                    if j == 0:
                        i_ = dve.tensor_scalar(C2[:, c, :], U2[:, c, 0:S], VT[:, c, 34:35], None, ALU.mult)
                    else:
                        dve.wait_ge(c2_n, 4 * (j - 1) + c + 1)
                        i_ = dve.scalar_tensor_tensor(out=C2[:, c, :], in0=U2[:, c, j:j + S], scalar=VT[:, c, 34 + j:35 + j],
                                                      in1=C2[:, c, :], op0=ALU.mult, op1=ALU.add)
                    i_.then_inc(c2_n, 1)
            dve.wait_ge(c2_n, 12)
            for m in range(8):
                if m == 7:
                    split_lo(B_W2)
                h, c = m // 4, m % 4
                cs = C2[:, c, h * 512:(h + 1) * 512]
                dve.wait_ge(acc_ready, T_BG + m + 1)
                dve.tensor_tensor(cs, cs, acc(T_BG + m), ALU.mult).then_inc(acc_dve, 1)
            for c in range(4):
                dve.wait_ge(c2_hi, c + 1)
                dve.tensor_tensor(AL[:, 4 + c, :], C2[:, c, :], AH[:, 4 + c, :], ALU.subtract).then_inc(c2_lo, 1)
            for v in range(64 + 7):
                if v < 64:
                    t, h = v // 8, v % 8
                    w = 640 if 0 < t < 7 else 512
                    dve.wait_ge(at_s, v + 1)
                    dlink(dve.tensor_reduce(M2[:, v:v + 1], PAIR[v % 2][:, 0:w], AX, ALU.max))
                    dve.tensor_scalar(NM2[:, v:v + 1], M2[:, v:v + 1], -AD ** -0.5, NSINK[:, h:h + 1], ALU.mult,
                                      ALU.min).then_inc(at_m, 1)
                if 2 <= v <= 65:
                    y = v - 2
                    w = 640 if 0 < y // 8 < 7 else 512
                    dve.wait_ge(at_t, y + 1)
                    if y >= 2:
                        dve.wait_ge(at_o, y - 1)
                    dve.tensor_copy(PT2[y % 2][:, 0:w], PAIR[2][:, 0:w]).then_inc(at_c, 1)
                if v >= 4 and (v - 4) % 8 == 7:
                    t = (v - 4) // 8
                    dve.wait_ge(at_o, 8 * t + 8)
                    dve.wait_ge(at_e, 8 * t + 8)
                    ls = L2[:, 8 * t:8 * t + 8]
                    dlink(dve.tensor_tensor(ls, ls, ES2[:, 8 * t:8 * t + 8], ALU.add))
                    dlink(dve.reciprocal(ls, ls))
                    if t >= 1:
                        dve.wait_ge(at_ot, t)
                    dve.tensor_tensor(OT[:, :].rearrange("p (h f) -> p h f", f=AD), BK[6 + t % 2].rearrange("p (h f) -> p h f", f=AD),
                                      ls.unsqueeze(2).to_broadcast([P, 8, AD]), ALU.mult).then_inc(at_on, 1)
                if v >= 6 and (v - 6) % 8 == 7:
                    t = (v - 6) // 8
                    dve.wait_ge(at_hi, t + 1)
                    dve.tensor_tensor(AL[:, 0:4, tok(t)], BK[6 + t % 2].rearrange("p (c n) -> p c n", c=4), AH[:, 0:4, tok(t)],
                                      ALU.subtract).then_inc(at_lo, 1)
            dve.wait_ge(mod_in, 64 + 64)
            dve.scalar_tensor_tensor(out=GAIN[:, :], in0=SCT[:, :], scalar=1.0, in1=GAIN[:, :], op0=ALU.add,
                                     op1=ALU.mult).then_inc(gain_made, 1)
            dve.wait_ge(gain_made, 3)

            def router_max(t):
                dve.wait_ge(rt_r, t + 1)
                dlink(dve.tensor_reduce(RST[:, 2, t:t + 1], BK[6 + t % 2][:, 0:NE], AX, ALU.max))
                dve.tensor_scalar(RST[:, 0, t:t + 1], RST[:, 2, t:t + 1], -1.0, None, ALU.mult).then_inc(rt_m, 1)

            def router_norm(t):
                dve.wait_ge(rt_e, t + 1)
                dlink(dve.reciprocal(RST[:, 3, t:t + 1], RST[:, 1, t:t + 1]))
                if t >= 2:
                    dve.wait_ge(rt_at, t - 1)
                dve.tensor_scalar(AFF[:, t % 2, :], REX[:, t % 2, :], RST[:, 3, t:t + 1], None, ALU.mult).then_inc(rt_a, 1)

            for half in range(2):
                for t in range(NT + (4 if half else 0)):
                    if t < NT:
                        if t == 7 and half == 0:
                            split_lo(B_W2 + 1)
                        n = T_W2 + 8 * half + t
                        dve.wait_ge(x2_in[t], 32)
                        dve.wait_ge(acc_ready, n + 1)
                        xs = X[:, t, 512 * half:512 * (half + 1)]
                        tmp = T1[:, n % 2, :]
                        dve.tensor_tensor(tmp, acc(n), GT1[:, 512 * half:512 * (half + 1)], ALU.mult).then_inc(acc_dve, 1)
                        dve.wait_ge(acc_dve, freed(n)[1])
                        i_ = dve.tensor_tensor(xs, xs, tmp, ALU.add)
                        if half == 1:
                            i_.then_inc(x3_new, 1)
                        else:
                            dlink(i_)
                    if half == 1:
                        if t < NT:
                            norm_rows(N_EXP + t, X[:, t, :], shift=SHIFT)
                        if 2 <= t < NT + 2:
                            router_max(t - 2)
                            router_norm(t - 2)
            dve.wait_ge(rt_ac, 8)
            for r in range(CAP // 8):
                v8 = TV[:, 8 * r:8 * r + 8]
                dlink(dve.max(out=v8, in_=AFT[:, :]))
                indexed = dve.max_index(out=TI[:, 8 * r:8 * r + 8], in_max=v8, in_values=AFT[:, :])
                if r < CAP // 8 - 1:
                    dlink(dve.match_replace(out=AFT[:, :], in_to_replace=v8, in_values=AFT[:, :], imm_value=-1.0))
            dlink(indexed)
            dve.tensor_copy(TIF[:, :], TI[:, :]).then_inc(tk, 1)
            dve.wait_ge(tk_tp, 1)
            dve.tensor_copy(GV[:, :], BK[6][:, 0:NE])
            dve.tensor_copy(GI[:, :], BK[6][:, 64:64 + NE]).then_inc(tk_out, 1)
            dve.wait_ge(tk_out, 1)
            dve.sem_inc(ex_y, 1)
            dve.wait_ge(gt2_in, 16)

            def expert_hidden(e, first=False):
                dve.wait_ge(ex_sg, e + 1)
                dve.wait_ge(ex_u, e + 1)
                if not first:
                    dve.wait_ge(ex_ht, e)
                dve.tensor_tensor(HE[:, :], SG[:, :], PAIR[1][:, :], ALU.mult).then_inc(ex_he, 1)

            def expert_y(e1):
                dve.wait_ge(ex_y, e1)
                dve.tensor_copy(GVC[:, :], GV[:, bass.ds(e1 - 1, 1)] if not isinstance(e1, int) else GV[:, e1 - 1:e1]).then_inc(ex_gv, 1)
                dve.wait_ge(ex_gv, e1)
                dve.wait_ge(ex_d, e1)
                dve.wait_ge(y_free, e1)
                dve.scalar_tensor_tensor(out=YE[:, :], in0=PAIR[2][:, :], scalar=GVC[:, 0:1], in1=GT2[:, :], op0=ALU.mult,
                                         op1=ALU.mult).then_inc(ex_y, 1)

            def expert_w_lo(slot, e):
                for j in range(2):
                    c = slice(2 * j, 2 * j + 2)
                    dve.wait_ge(w_hi, 8 * e + (W_SPLIT + 2 * slot + j + 1))
                    dve.tensor_tensor(EWL[slot][:, c, :], EW[slot][:, c, :], EWH[slot][:, c, :], ALU.subtract).then_inc(w_ready, 1)

            def expert_rows_lo(e):
                dve.wait_ge(ex_xc, e + 1)
                dve.tensor_tensor(XTL[:, :, :], PAIR[3][:, :].rearrange("p (c n) -> p c n", c=8), XTH[:, :, :],
                                  ALU.subtract).then_inc(ex_xl, 1)

            def expert_dve(e, first=False, more=True):
                if more:
                    expert_w_lo(0, e + 1)
                expert_hidden(e, first)
                if more:
                    expert_w_lo(1, e + 1)
                    expert_rows_lo(e + 1)
                    expert_w_lo(2, e + 1)
                    expert_w_lo(3, e + 1)
                if not first:
                    expert_y(e)

            expert_w_lo(0, 0)
            expert_rows_lo(0)
            for slot in range(1, 4):
                expert_w_lo(slot, 0)
            expert_dve(0, first=True)
            with dve.Fori(1, NE - 1) as e:
                expert_dve(e)
            expert_dve(NE - 1, more=False)
            expert_y(NE)
            dve.wait_ge(gain_in, 80)
            for t in range(NT):
                plain_rows(8 + t, X[:, t, :])

        @block.tensor
        def _(pe):
            pe.wait_ge(cst_in, 16)
            for t in range(NT):
                norm_transpose(N_MIX + t)
            pe.wait_ge(vec_in, 16 * 9)
            pe.transpose(BK[0][:, 0:16], C8[:, :], CST[0:16, CI:CI + 16]).then_inc(c_tp, 1)
            for c in range(4):
                m = pe.transpose(BK[1][:, 37 * c:37 * (c + 1)], VEC[:, c * P:(c + 1) * P], CST[0:37, CI:CI + 37])
            m.then_inc(vt_tp, 1)
            pe.wait_ge(c_silu, 1)
            pe.wait_ge(vt_sb, 1)
            pe.wait_ge(nm_lo, 16)
            gemm_features(0, T_CB)
            gemm_features(1, T_CA)
            gemm_tokens(2, T_QK)
            gemm_tokens(3, T_V)
            gemm_tokens(4, T_G)
            def ada_step(n):
                j, half = n // 2, n % 2
                if half == 0:
                    if j >= 2:
                        pe.wait_ge(mod_made, j - 1)
                    pe.wait_ge(bias_in[j % 2], 16 * (j // 2 + 1))
                    pe.matmul(BK[2 + j % 2][0:2, :], RC[0:1, RB:RB + 2], BIAS[:, j % 2, :], start=True, stop=False)
                pe.wait_ge(ada_in[half], 16 * (j + 1))
                for k in range(4):
                    m = pe.matmul(BK[2 + j % 2][0:2, :], CS[:, :, 4 * half + k], raw[:, half, k, :], start=False,
                                  stop=(half == 1 and k == 3))
                m.then_inc(ada_acc, 1)

            pe.wait_ge(ret_in, 32)
            for t in range(NT):
                if t >= 1:
                    pe.wait_ge(ret_q, t)
                    pe.wait_ge(ret_k, t)
                else:
                    pe.wait_ge(acc_dve, freed(T_QK + 7)[1])
                for n in range(4):
                    m = pe.transpose(BK[4][:, n * P:(n + 1) * P], QK[:, t, n * P:(n + 1) * P], IDN)
                m.then_inc(ret_tp, 1)
                if t == 0:
                    pe.wait_ge(acc_act, freed(T_G + 7)[1])
                ada_step(3 * t)
                pe.wait_ge(ret_q, t + 1)
                pe.wait_ge(ret_k, t + 1)
                for g in range(2):
                    m = pe.matmul(BK[5 + g][:, :], KTT[:, g, :], QBD[:, g, :, :].rearrange("p h n -> p (h n)"), start=True, stop=True)
                m.then_inc(ret_s, 1)
                if t >= 1:
                    pe.wait_ge(ret_state, t + 1)
                for g in range(2):
                    m = pe.matmul(BK[0][:, 256 * g:256 * (g + 1)], KZ[:, g * P:(g + 1) * P], V[:, t, 256 * g:256 * (g + 1)],
                                  start=(g == 0), stop=(g == 1), skip_group_check=True)
                m.then_inc(ret_kv, 1)
                pe.wait_ge(ret_state, t + 1)
                if t >= 1:
                    pe.wait_ge(ret_d, t)
                for g in range(2):
                    pe.matmul(BK[7][:, 256 * g:256 * (g + 1)], QX[:, g, :], STATE[:, g, :], start=(g == 0), stop=False,
                              skip_group_check=True)
                pe.wait_ge(ret_st, t + 1)
                for h in range(HR):
                    m = pe.matmul(BK[7][:, DV * h:DV * (h + 1)], ST[:, h, :], V[:, t, DV * h:DV * (h + 1)],
                                  start=False, stop=(h == HR - 1), skip_group_check=True)
                m.then_inc(ret_y, 1)
                ada_step(3 * t + 1)
                ada_step(3 * t + 2)
                pe.wait_ge(ret_yn, 2 * t + 2)
                if t >= 1:
                    pe.wait_ge(ret_lo, t)
                for n in range(4):
                    m = pe.transpose(BK[1][:, n * P:(n + 1) * P], YD[:, n * P:(n + 1) * P], IDN)
                m.then_inc(ret_ty, 1)
            pe.wait_ge(conv_n, 4 * TAPS)
            pe.wait_ge(mod_made, ADA_STEPS // 2)
            for h in range(2):
                for c in range(4):
                    m = pe.matmul(BK[2 + h][:, :], ONESM, YC[:, c, h * 512:(h + 1) * 512], start=(c == 0), stop=(c == 3))
                m.then_inc(ln_mean, 1)
            pe.wait_ge(ln_d, 8)
            pe.wait_ge(ln_sq, 4)
            for h in range(2):
                for c in range(4):
                    m = pe.matmul(BK[2 + h][:, :], ONESM, SQ[:, c, h * 512:(h + 1) * 512], start=(c == 0), stop=(c == 3))
                m.then_inc(ln_var, 1)
            pe.wait_ge(ln_lo, 4)
            pe.wait_ge(ret_lo, 8)
            residual_pe(B_WO, T_WO, N_XAT)
            for m in range(2):
                norm_transpose(N_MEM + m)
            pe.wait_ge(nm_lo, 2 * (N_MEM + 2))
            for kb in range(2):
                b = B_KV + kb
                for c in range(4):
                    n = T_MK + 4 * kb + c
                    wait_acc_free(n)
                    for k in range(8):
                        if c == 0 and k % 2 == 0:
                            pe.wait_ge(w_ready, 4 * b + k // 2 + 1)
                        m = mm3(acc(n)[:, 0:MEM], WH[:, k, c * P:(c + 1) * P], WL[:, k, c * P:(c + 1) * P], MTH[:, k, :],
                                MTL[:, k, :], k == 0, k == 7)
                        if c == 3 and k in (1, 3, 5):
                            m.then_inc(w_used, 1)
                    m.then_inc(acc_ready, 1)

            def mem_lhs(t):
                return MTH[:, :, tok(t)], MTL[:, :, tok(t)]

            for vb in range(2):
                gemm_tokens(B_KV + 2 + vb, T_MV + 2 * vb, hi=2, lhs=mem_lhs)
            for qb in range(2):
                gemm_features(B_XQ + qb, T_XQ + 8 * qb)
            pe.wait_ge(acc_act, freed(T_XQ + 15)[1])
            for u in range(16 + 2):
                if u < 16:
                    t, hp = u // 2, u % 2
                    if u >= 2:
                        pe.wait_ge(xa_e, u - 1)
                    for hh in range(2):
                        for dd in range(2):
                            f = 2 * (2 * hp + hh) + dd
                            m = pe.matmul(BK[4 + u % 2][:, 256 * hh:256 * (hh + 1)], QT[:, f, tok(t)], KX[:, f, :],
                                          start=(dd == 0), stop=(dd == 1))
                    m.then_inc(xa_s, 1)
                if 1 <= u <= 16:
                    w = u - 1
                    pe.wait_ge(xa_p, w + 1)
                    if w >= 2:
                        pe.wait_ge(xa_pt, w - 1)
                    for n in range(4):
                        m = pe.transpose(BK[6 + w % 2][:, n * P:(n + 1) * P], PX[:, w % 2, n * P:(n + 1) * P], IDN)
                    m.then_inc(xa_t, 1)
                if u >= 2:
                    w = u - 2
                    hp = w % 2
                    pe.wait_ge(xa_pt, w + 1)
                    if w >= 4:
                        pe.wait_ge(xa_lo, w - 3)
                    for hh in range(2):
                        for dd in range(2):
                            col = 256 * (2 * hp + hh) + P * dd
                            for mm in range(2):
                                m = pe.matmul(BK[w % 4][:, (2 * hh + dd) * P:(2 * hh + dd + 1) * P], VX[:, mm, col:col + P],
                                              PT[:, w % 2, 2 * hh + mm, :], start=(mm == 0), stop=(mm == 1))
                    m.then_inc(xa_o, 1)
            pe.wait_ge(xa_lo, 16)
            residual_pe(B_XO, T_XO, N_MLP)
            pe.wait_ge(nm_lo, 2 * (N_MLP + 8))
            def mlp_block(f, after=None):
                gemm_features(B_ML, T_ML, off=2 * f)
                for q in range(16):
                    t, half = q // 2, q % 2
                    n = T_ML + 8 + q
                    if q == 0:
                        pe.wait_ge(u_lo, f * 8 + 6)
                    if q == 8:
                        pe.wait_ge(u_lo, f * 8 + 10)
                    wait_acc_free(n, 2 * f)
                    for k in range(4):
                        if q == 0:
                            pe.wait_ge(w_ready, f * 8 + 4 * (B_ML + 1) + k + 1)
                        ch = 2 * k + half
                        m = mm3(acc(n), UH[:, k, tok(t)], UL[:, k, tok(t)], WH[:, ch, :], WL[:, ch, :], k == 0, k == 3)
                        if q == 15 and k < 3:
                            m.then_inc(w_used, 1)
                    m.then_inc(acc_ready, 1)
                    if after is not None and half == 1:
                        after(t)

            with pe.Fori(0, NFB - 1) as f:
                mlp_block(f)
            mlp_block(NFB - 1, after=lambda t: norm_transpose(N_B2 + t - 3) if t >= 3 else None)
            for t in range(NT - 3, NT):
                norm_transpose(N_B2 + t)
            pe.wait_ge(nm_lo, 2 * (N_B2 + NT))

            def rot_transpose(r):
                n = (T_Q2 if r < 8 else T_KV - 8) + r
                pe.wait_ge(acc_dve, freed(n)[1])
                if r >= 4:
                    pe.wait_ge(rt_cp, r - 3)
                for c in range(4 if r < 8 else 2):
                    m = pe.transpose(BK[4 + r % 4][:, c * P:(c + 1) * P], QR[:, r % 2, c * P:(c + 1) * P], IDN)
                m.then_inc(rt_tp, 1)

            def beside_queries(t):
                if t < 2:
                    norm_transpose(N_CTX + t)
                if t == 2:
                    pe.wait_ge(nm_lo, 2 * (N_CTX + 2))
                    rot_transpose(0)
                if t >= 2:
                    rot_transpose(t - 1)

            gemm_tokens(B_I2, T_Q2, after=beside_queries)

            def kv_lhs(i):
                return mem_lhs(i) if i < 2 else (AH[:, :, tok(i - 2)], AL[:, :, tok(i - 2)])

            gemm_tokens(B_I2 + 1, T_KV, hi=10, lhs=kv_lhs, rhs_cols=(0, 256), after=lambda i: rot_transpose(7 + i))
            rot_transpose(17)
            gemm_features(B_I2 + 2, T_CG)
            gemm_features(B_I2 + 3, T_HV)
            gemm_features(B_I2 + 4, T_BG)
            pe.wait_ge(rt_cp, 18)
            pe.wait_ge(acc_dve, freed(T_BG + 7)[1])
            for v in range(64 + 6):
                if v < 64:
                    t, h = v // 8, v % 8
                    if v >= 2:
                        pe.wait_ge(at_e, v - 1)
                    ps = PAIR[v % 2]
                    q = QT2[:, h // 2, tok(t)]
                    kz = KZ4[:, 2 * (h // 4) + h % 2, :]
                    pe.matmul(ps[:, 0:CTX], q, kz[:, 0:CTX], start=True, stop=True)
                    m = pe.matmul(ps[:, CTX:CTX + P], q, kz[:, CTX + t * P:CTX + (t + 1) * P], start=True, stop=True)
                    sides = ([(t - 1, 0)] if t > 0 else []) + ([(t + 1, 1)] if t < NT - 1 else [])
                    for n, (kt, side) in enumerate(sides):
                        dst = ps[:, CTX + P * (n + 1):CTX + P * (n + 2)]
                        pe.matmul(dst, q, kz[:, CTX + kt * P:CTX + (kt + 1) * P], start=True, stop=False)
                        m = pe.matmul(dst, IDB[:, :], MKB[:, side, :], start=False, stop=True)
                    m.then_inc(at_s, 1)
                if 2 <= v <= 65:
                    y = v - 2
                    pe.wait_ge(at_e, y + 1)
                    if y >= 1:
                        pe.wait_ge(at_c, y)
                    for n in range(5 if 0 < y // 8 < 7 else 4):
                        m = pe.transpose(PAIR[2][:, n * P:(n + 1) * P], P2[:, y % 2, n * P:(n + 1) * P], IDN)
                    m.then_inc(at_t, 1)
                if 3 <= v <= 66:
                    y = v - 3
                    t, h = y // 8, y % 8
                    pe.wait_ge(at_c, y + 1)
                    if h == 0 and t >= 2:
                        pe.wait_ge(at_lo, t - 1)
                    keys = [0, 1, 2 + t] + ([1 + t] if t > 0 else []) + ([3 + t] if t < NT - 1 else [])
                    for n, kt in enumerate(keys):
                        m = pe.matmul(BK[6 + t % 2][:, AD * h:AD * (h + 1)], PT2[y % 2][:, n * P:(n + 1) * P],
                                      V2[:, kt, 64 * (h // 4):64 * (h // 4) + 64], start=(n == 0), stop=(n == len(keys) - 1))
                    m.then_inc(at_o, 1)
                if v >= 5 and (v - 5) % 8 == 7:
                    t = (v - 5) // 8
                    pe.wait_ge(at_on, t + 1)
                    for n in range(4):
                        m = pe.transpose(BK[6 + t % 2][:, n * P:(n + 1) * P], OT[:, n * P:(n + 1) * P], IDN)
                    m.then_inc(at_ot, 1)
            pe.wait_ge(at_lo, 8)
            pe.wait_ge(c2_lo, 4)
            gemm_tokens(B_W2, T_W2)

            def router(t):
                pe.wait_ge(nm_hi, 2 * (N_EXP + t) + 2)
                if t >= 2:
                    pe.wait_ge(rt_ac, t - 1)
                else:
                    pe.wait_ge(wr_in, 16)
                for k in range(8):
                    m = pe.matmul(BK[6 + t % 2][:, 0:NE], HTR[:, t % 2, k, :], WR[:, k, :], start=(k == 0), stop=(k == 7))
                m.then_inc(rt_r, 1)

            def aff_transpose(t):
                pe.wait_ge(rt_a, t + 1)
                pe.transpose(BK[6 + t % 2][0:NE, P:2 * P], AFF[:, t % 2, :], IDN).then_inc(rt_at, 1)

            def route(t):
                if 1 <= t <= NT:
                    norm_transpose(N_EXP + t - 1, banks=2, free=nm_hi)
                if 2 <= t < NT + 2:
                    router(t - 2)
                if 3 <= t < NT + 3:
                    aff_transpose(t - 3)

            gemm_tokens(B_W2 + 1, T_W2 + 8, after=route)
            for t in range(NT, NT + 3):
                route(t)
            pe.wait_ge(tk, 1)
            pe.transpose(BK[6][:, 0:NE], TV[:, :], CST[0:NE, CI:CI + NE])
            pe.transpose(BK[6][:, 64:64 + NE], TIF[:, :], CST[0:NE, CI:CI + NE]).then_inc(tk_tp, 1)

            def rows_T(e):
                pe.wait_ge(xs_in, 16 * e + 16)
                for k in range(8):
                    m = pe.transpose(PAIR[3][:, k * P:(k + 1) * P], XS[:, k * P:(k + 1) * P], IDN)
                m.then_inc(ex_xt, 1)

            def product(pair, lhs, slot, e, full, half_done):
                for k in range(8):
                    if k % 4 == 0:
                        pe.wait_ge(ew_in[slot + k // 4], 16 * e + 16)
                    for half in range(2):
                        m = pe.matmul(PAIR[pair][:, 512 * half:512 * (half + 1)], lhs[:, k, :],
                                      EW[slot + k // 4][:, k % 4, 512 * half:512 * (half + 1)], start=(k == 0), stop=(k == 7))
                    if k == 3:
                        m.then_inc(half_done, 1)
                m.then_inc(full, 1)

            def split_product(pair, slot, e, full, half_done):
                for k in range(8):
                    w = slot + k // 4
                    if k % 2 == 0:
                        pe.wait_ge(w_ready, 8 * e + (W_SPLIT + 2 * slot + k // 2 + 1))
                    for half in range(2):
                        c = slice(512 * half, 512 * (half + 1))
                        m = mm3(PAIR[pair][:, c], XTH[:, k, :], XTL[:, k, :], EWH[w][:, k % 4, c], EWL[w][:, k % 4, c], k == 0, k == 7)
                    if k == 3:
                        m.then_inc(half_done, 1)
                m.then_inc(full, 1)

            def gate_up(e, first=False):
                pe.wait_ge(ex_xl, e + 1)
                if not first:
                    pe.wait_ge(ex_sg, e)
                split_product(0, 0, e, ex_g, ew_half[0])
                if not first:
                    pe.wait_ge(ex_he, e)
                split_product(1, 2, e, ex_u, ew_half[1])

            def down(e1):
                pe.wait_ge(ex_hc, e1)
                pe.wait_ge(ex_y, e1)
                product(2, HTE, 4, e1 - 1, ex_d, ew_half[2])

            def hidden_T(e, copies):
                pe.wait_ge(ex_he, e + 1)
                pe.wait_ge(ex_xl, copies)
                for k in range(8):
                    m = pe.transpose(PAIR[3][:, k * P:(k + 1) * P], HE[:, k * P:(k + 1) * P], IDN)
                m.then_inc(ex_ht, 1)

            pe.wait_ge(tk_out, 1)
            rows_T(0)
            gate_up(0, first=True)
            pe.wait_ge(ex_xl, 1)
            rows_T(1)
            hidden_T(0, 2)
            with pe.Fori(1, NE - 1) as e:
                gate_up(e)
                pe.wait_ge(ex_hc, e)
                rows_T(e + 1)
                down(e)
                hidden_T(e, e + 2)
            gate_up(NE - 1)
            down(NE - 1)
            hidden_T(NE - 1, NE)
            down(NE)


NAMES = ["x", "mem", "positions", "norm_mix_w", "w_in", "conv_w", "conv_b", "conv_ln_w", "conv_ln_b", "ret_gn_w", "w_out",
         "norm_xattn_w", "norm_mem_w", "xq_w", "xkv_w", "xo_w", "norm_mlp_w", "mlp_up_w", "mlp_down_w", "norm_f_w",
         "c_2", "ctx_2", "c_ctx_2", "w_ada_2", "b_ada_2", "g_mix_2", "w_in_2", "conv_w_2", "sink_2", "w_out_2", "g_ffn_2",
         "w_router_2", "w_gate_2", "w_up_2", "w_down_2", "g_final_2"]


def kernel(**inputs):
    import concourse.bacc as bacc
    from concourse.bass_utils import run_bass_kernel_spmd

    nc = bacc.Bacc("TRN2", target_bir_lowering=False, num_devices=1)
    arrays, args = {}, {}
    c, r = shape_constants()
    for name, a in [(n, np.ascontiguousarray(inputs[n])) for n in NAMES] + [("consts", c), ("rconsts", r)]:
        arrays["in_" + name] = a
        args[name] = nc.dram_tensor("in_" + name, a.shape, mybir.dt.from_np(a.dtype), kind="ExternalInput").ap()
    out = nc.dram_tensor("out_0", (1, S, D), F32, kind="ExternalOutput").ap()
    build(nc, **args, out=out)
    return run_bass_kernel_spmd(nc, [arrays], core_ids=[0]).results[0]["out_0"]
```
